# Optimizing a Trainium2 kernel written in Bass

```python
import math
import jax, jax.numpy as jnp
from jax import lax
import numpy as np

D_MODEL = 1024
BATCH = 1
SEQ = 512
DEPTH = 2

CHUNK = 64
RMS_EPS = 1e-6

SSM_GROUP = 16
SSM_WIDTH = D_MODEL // 4
SSM_GROUPS = SSM_WIDTH // SSM_GROUP
SSM_STATE = 64
GMLP_HEADS = 4
GMLP_HEAD_DIM = 64
GMLP_WIDTH = GMLP_HEADS * GMLP_HEAD_DIM
GMLP_BLOCK = 128
ATT_HEADS = 8
ATT_HEAD_DIM = 64
ATT_WIDTH = ATT_HEADS * ATT_HEAD_DIM
KV_RANK = 128
IDX_HEADS = 4
IDX_DIM = 64
TOPK_MAX = 256
Q_BLOCK = 128

MIX_WIDTH = SSM_WIDTH + GMLP_WIDTH + ATT_WIDTH

IN_SIZES = (SSM_WIDTH, GMLP_WIDTH, GMLP_WIDTH, ATT_WIDTH, KV_RANK, IDX_HEADS * IDX_DIM, IDX_DIM, IDX_HEADS)
IN_WIDTH = sum(IN_SIZES)
IN_SPLITS = [sum(IN_SIZES[:i + 1]) for i in range(len(IN_SIZES) - 1)]

PEER_HEADS = 8
PEER_KEY_DIM = 128
PEER_N_KEYS = 128
PEER_N_EXPERTS = PEER_N_KEYS * PEER_N_KEYS
PEER_TOPK = 16
PEER_TOKEN_BLOCK = 128

kernel_name = "hybrid_s5_gmlp_dsa_peer_adaln"

def rms_norm(x, g):
    xf = x.astype(jnp.float32)
    y = xf * lax.rsqrt(jnp.mean(xf * xf, axis=-1, keepdims=True) + RMS_EPS)
    return (y * g.astype(jnp.float32)).astype(x.dtype)

def ssm_mixer(u, a_re_log, a_im, b_re, b_im, c_re, c_im, d_skip, log_dt, w_glu, b_glu):
    f32 = jnp.float32
    Bsz, L, _ = u.shape
    uf = u.astype(f32)
    ug = uf.reshape(Bsz, L, SSM_GROUPS, SSM_GROUP)
    lam_re = -jnp.exp(a_re_log.astype(f32))
    lam_im = a_im.astype(f32)
    dt = jnp.exp(log_dt.astype(f32))[:, None]
    mag = jnp.exp(lam_re * dt)
    abar_re = mag * jnp.cos(lam_im * dt)
    abar_im = mag * jnp.sin(lam_im * dt)
    den = lam_re * lam_re + lam_im * lam_im
    p = abar_re - 1.0
    q = abar_im
    f_re = (p * lam_re + q * lam_im) / den
    f_im = (q * lam_re - p * lam_im) / den
    br = b_re.astype(f32)
    bi = b_im.astype(f32)
    bb_re = f_re[..., None] * br - f_im[..., None] * bi
    bb_im = f_re[..., None] * bi + f_im[..., None] * br
    bu_re = jnp.einsum('gph,blgh->blgp', bb_re, ug)
    bu_im = jnp.einsum('gph,blgh->blgp', bb_im, ug)
    a_re_t = jnp.broadcast_to(abar_re, bu_re.shape)
    a_im_t = jnp.broadcast_to(abar_im, bu_re.shape)

    def combine(left, right):
        a1r, a1i, b1r, b1i = left
        a2r, a2i, b2r, b2i = right
        return (a1r * a2r - a1i * a2i,
                a1r * a2i + a1i * a2r,
                a2r * b1r - a2i * b1i + b2r,
                a2r * b1i + a2i * b1r + b2i)

    _, _, s_re, s_im = lax.associative_scan(combine, (a_re_t, a_im_t, bu_re, bu_im), axis=1)
    y = (jnp.einsum('ghp,blgp->blgh', c_re.astype(f32), s_re)
         - jnp.einsum('ghp,blgp->blgh', c_im.astype(f32), s_im))
    y = y.reshape(Bsz, L, SSM_WIDTH) + d_skip.astype(f32) * uf
    yg = jax.nn.gelu(y)
    out = yg * jax.nn.sigmoid(yg @ w_glu.astype(f32) + b_glu.astype(f32))
    return out.astype(u.dtype)

def gmlp_mixer(u, v, w_sp, b_sp):
    Bsz, L, _ = u.shape
    nb = L // GMLP_BLOCK
    vf = v.reshape(Bsz, nb, GMLP_BLOCK, GMLP_HEADS, GMLP_HEAD_DIM).astype(jnp.float32)
    mu = jnp.mean(vf, axis=-1, keepdims=True)
    var = jnp.mean(jnp.square(vf - mu), axis=-1, keepdims=True)
    vn = ((vf - mu) * lax.rsqrt(var + RMS_EPS)).astype(v.dtype)
    chunk_id = jnp.arange(GMLP_BLOCK) // CHUNK
    mask = chunk_id[:, None] >= chunk_id[None, :]
    w = jnp.where(mask[None], w_sp, 0.0)
    mixed = jnp.einsum('hts,bnshd->bnthd', w, vn) + b_sp.T[None, None, :, :, None]
    out = u.reshape(Bsz, nb, GMLP_BLOCK, GMLP_HEADS, GMLP_HEAD_DIM) * mixed
    return out.reshape(Bsz, L, GMLP_WIDTH)

def dsa_mixer(q, c_kv, q_idx, k_idx, w_idx, w_uk, w_uv):
    f32 = jnp.float32
    Bsz, L = q.shape[0], q.shape[1]
    topk = min(TOPK_MAX, L // 4)
    nqb = L // Q_BLOCK
    slopes = jnp.exp2(-8.0 * (jnp.arange(ATT_HEADS, dtype=f32) + 1.0) / ATT_HEADS)
    q_abs = jnp.einsum('blhd,hdr->blhr', q, w_uk) * (ATT_HEAD_DIM ** -0.5)
    w_scaled = w_idx * (IDX_HEADS ** -0.5)
    key_chunk = jnp.arange(L) // CHUNK
    b_ix = jnp.arange(Bsz)[:, None, None]

    def to_blocks(a):
        return jnp.moveaxis(a.reshape((Bsz, nqb, Q_BLOCK) + a.shape[2:]), 1, 0)

    def block_fn(args):
        qa, qi, wi, qpos = args
        s = jnp.einsum('bthd,bsd->bths', qi, k_idx) * (IDX_DIM ** -0.5)
        score = jnp.einsum('bth,bths->bts', wi, jax.nn.relu(s)).astype(f32)
        adm = key_chunk[None, :] <= (qpos // CHUNK)[:, None]
        score = jnp.where(adm[None], score, -jnp.inf)
        sel_score, sel = lax.top_k(score, topk)
        valid = jnp.isfinite(sel_score)
        kv = c_kv[b_ix, sel]
        logits = jnp.einsum('bthr,btkr->bthk', qa, kv).astype(f32)
        dist = jnp.abs(qpos[None, :, None] - sel).astype(f32)
        logits = logits - slopes[None, None, :, None] * dist[:, :, None, :]
        logits = jnp.where(valid[:, :, None, :], logits, -jnp.inf)
        probs = jax.nn.softmax(logits, axis=-1).astype(kv.dtype)
        return jnp.einsum('bthk,btkr->bthr', probs, kv)

    qpos_blocks = jnp.arange(L).reshape(nqb, Q_BLOCK)
    o = lax.map(block_fn, (to_blocks(q_abs), to_blocks(q_idx), to_blocks(w_scaled), qpos_blocks))
    o = jnp.moveaxis(o, 0, 1).reshape(Bsz, L, ATT_HEADS, KV_RANK)
    out = jnp.einsum('blhr,hrd->blhd', o, w_uv)
    return out.reshape(Bsz, L, ATT_WIDTH)

def peer_ffn(h, w_q, sub_k1, sub_k2, peer_u, peer_v):
    f32 = jnp.float32
    Bsz, L, D = h.shape
    half = PEER_KEY_DIM // 2
    q = (h @ w_q).reshape(Bsz, L, PEER_HEADS, 2, half)
    s1 = jnp.einsum('blhd,nd->blhn', q[..., 0, :], sub_k1).astype(f32)
    s2 = jnp.einsum('blhd,nd->blhn', q[..., 1, :], sub_k2).astype(f32)
    v1, i1 = lax.top_k(s1, PEER_TOPK)
    v2, i2 = lax.top_k(s2, PEER_TOPK)
    ncand = PEER_TOPK * PEER_TOPK
    cand = (v1[..., :, None] + v2[..., None, :]).reshape(Bsz, L, PEER_HEADS, ncand)
    cand_idx = (i1[..., :, None] * PEER_N_KEYS + i2[..., None, :]).reshape(Bsz, L, PEER_HEADS, ncand)
    top_s, pos = lax.top_k(cand, PEER_TOPK)
    experts = jnp.take_along_axis(cand_idx, pos, axis=-1)
    gates = jax.nn.softmax(top_s, axis=-1).astype(h.dtype)
    n_tok = Bsz * L
    nb = n_tok // PEER_TOKEN_BLOCK
    hk = PEER_HEADS * PEER_TOPK
    hb = h.reshape(nb, PEER_TOKEN_BLOCK, D)
    eb = experts.reshape(nb, PEER_TOKEN_BLOCK, hk)
    gb = gates.reshape(nb, PEER_TOKEN_BLOCK, hk)

    def block_fn(args):
        hx, e, g = args
        act = jax.nn.gelu(jnp.einsum('tkd,td->tk', peer_u[e], hx))
        return jnp.einsum('tk,tkd->td', g * act, peer_v[e])

    out = lax.map(block_fn, (hb, eb, gb))
    return out.reshape(Bsz, L, D)

def setup_inputs(seed: int = 0) -> dict:
    key = jax.random.key(seed)
    ks = iter(jax.random.split(key, 40))
    D = D_MODEL
    NL = DEPTH

    def nrm(shape, scale):
        return jax.random.normal(next(ks), shape, jnp.float32) * scale

    x = nrm((BATCH, SEQ, D), 1.0)
    c = nrm((BATCH, D), 1.0)
    norm1_g = 1.0 + nrm((NL, D), 0.02)
    norm2_g = 1.0 + nrm((NL, D), 0.02)
    w_mod = nrm((NL, D, 6 * D), 0.5 * D ** -0.5)
    b_mod = nrm((NL, 6 * D), 0.02)
    w_in = nrm((NL, D, IN_WIDTH), D ** -0.5)
    ssm_a_re_log = math.log(0.5) + nrm((NL, SSM_GROUPS, SSM_STATE), 0.01)
    ssm_a_im = math.pi * jnp.arange(SSM_STATE, dtype=jnp.float32)[None, None, :] + nrm((NL, SSM_GROUPS, SSM_STATE), 0.01)
    ssm_b_re = nrm((NL, SSM_GROUPS, SSM_STATE, SSM_GROUP), (2 * SSM_GROUP) ** -0.5)
    ssm_b_im = nrm((NL, SSM_GROUPS, SSM_STATE, SSM_GROUP), (2 * SSM_GROUP) ** -0.5)
    ssm_c_re = nrm((NL, SSM_GROUPS, SSM_GROUP, SSM_STATE), 2.0 * SSM_STATE ** -0.5)
    ssm_c_im = nrm((NL, SSM_GROUPS, SSM_GROUP, SSM_STATE), 2.0 * SSM_STATE ** -0.5)
    ssm_d = nrm((NL, SSM_WIDTH), 0.5)
    ssm_log_dt = jax.random.uniform(next(ks), (NL, SSM_GROUPS), jnp.float32, math.log(1e-3), math.log(1e-1))
    ssm_w_glu = nrm((NL, SSM_WIDTH, SSM_WIDTH), SSM_WIDTH ** -0.5)
    ssm_b_glu = nrm((NL, SSM_WIDTH), 0.02)
    gmlp_w_sp = nrm((NL, GMLP_HEADS, GMLP_BLOCK, GMLP_BLOCK), 0.05)
    gmlp_b_sp = 1.0 + nrm((NL, GMLP_HEADS, GMLP_BLOCK), 0.02)
    kv_norm_g = 1.0 + nrm((NL, KV_RANK), 0.02)
    w_uk = nrm((NL, ATT_HEADS, ATT_HEAD_DIM, KV_RANK), KV_RANK ** -0.5)
    w_uv = nrm((NL, ATT_HEADS, KV_RANK, ATT_HEAD_DIM), KV_RANK ** -0.5)
    w_out = nrm((NL, MIX_WIDTH, D), MIX_WIDTH ** -0.5)
    peer_w_q = nrm((NL, D, PEER_HEADS * PEER_KEY_DIM), D ** -0.5)
    peer_k1 = nrm((NL, PEER_N_KEYS, PEER_KEY_DIM // 2), (PEER_KEY_DIM // 2) ** -0.5)
    peer_k2 = nrm((NL, PEER_N_KEYS, PEER_KEY_DIM // 2), (PEER_KEY_DIM // 2) ** -0.5)
    peer_u = nrm((NL, PEER_N_EXPERTS, D), D ** -0.5)
    peer_v = nrm((NL, PEER_N_EXPERTS, D), 0.3)
    final_g = 1.0 + nrm((D,), 0.02)
    return {"x": x, "c": c, "norm1_g": norm1_g, "norm2_g": norm2_g, "w_mod": w_mod, "b_mod": b_mod,
            "w_in": w_in, "ssm_a_re_log": ssm_a_re_log, "ssm_a_im": ssm_a_im, "ssm_b_re": ssm_b_re,
            "ssm_b_im": ssm_b_im, "ssm_c_re": ssm_c_re, "ssm_c_im": ssm_c_im, "ssm_d": ssm_d,
            "ssm_log_dt": ssm_log_dt, "ssm_w_glu": ssm_w_glu, "ssm_b_glu": ssm_b_glu,
            "gmlp_w_sp": gmlp_w_sp, "gmlp_b_sp": gmlp_b_sp, "kv_norm_g": kv_norm_g, "w_uk": w_uk,
            "w_uv": w_uv, "w_out": w_out, "peer_w_q": peer_w_q, "peer_k1": peer_k1, "peer_k2": peer_k2,
            "peer_u": peer_u, "peer_v": peer_v, "final_g": final_g}

def reference(x, c, norm1_g, norm2_g, w_mod, b_mod, w_in, ssm_a_re_log, ssm_a_im, ssm_b_re, ssm_b_im,
              ssm_c_re, ssm_c_im, ssm_d, ssm_log_dt, ssm_w_glu, ssm_b_glu, gmlp_w_sp, gmlp_b_sp,
              kv_norm_g, w_uk, w_uv, w_out, peer_w_q, peer_k1, peer_k2, peer_u, peer_v, final_g):
    Bsz, L, _ = x.shape
    c_act = jax.nn.silu(c)
    for l in range(DEPTH):
        mod = c_act @ w_mod[l] + b_mod[l]
        sh1, sc1, g1, sh2, sc2, g2 = jnp.split(mod[:, None, :], 6, axis=-1)
        h = rms_norm(x, norm1_g[l]) * (1.0 + sc1) + sh1
        proj = h @ w_in[l]
        u_a, u_b, v_b, q, ckv, qi, ki, wi = jnp.split(proj, IN_SPLITS, axis=-1)
        y_a = ssm_mixer(u_a, ssm_a_re_log[l], ssm_a_im[l], ssm_b_re[l], ssm_b_im[l], ssm_c_re[l],
                        ssm_c_im[l], ssm_d[l], ssm_log_dt[l], ssm_w_glu[l], ssm_b_glu[l])
        y_b = gmlp_mixer(u_b, v_b, gmlp_w_sp[l], gmlp_b_sp[l])
        y_c = dsa_mixer(q.reshape(Bsz, L, ATT_HEADS, ATT_HEAD_DIM), rms_norm(ckv, kv_norm_g[l]),
                        qi.reshape(Bsz, L, IDX_HEADS, IDX_DIM), ki, wi, w_uk[l], w_uv[l])
        mix = jnp.concatenate([y_a, y_b, y_c], axis=-1)
        x = x + g1 * (mix @ w_out[l])
        h = rms_norm(x, norm2_g[l]) * (1.0 + sc2) + sh2
        x = x + g2 * peer_ffn(h, peer_w_q[l], peer_k1[l], peer_k2[l], peer_u[l], peer_v[l])
    return rms_norm(x, final_g)


_drawn_inputs = setup_inputs


def setup_inputs(seed=0):
    import zlib

    import numpy as np

    out = dict(_drawn_inputs(seed))
    spreads = {}
    factors = {'norm2_g': 4.541,
     'ssm_a_re_log': 64.0,
     'ssm_a_im': 3.188,
     'ssm_b_re': 3.951,
     'ssm_b_im': 4.426,
     'ssm_c_re': 11.869,
     'ssm_c_im': 10.66,
     'ssm_log_dt': 3.597,
     'ssm_w_glu': 5.136,
     'ssm_b_glu': 24.69,
     'gmlp_b_sp': 7.116,
     'kv_norm_g': 7.329,
     'final_g': 19.527}
    for name, (base, spread) in spreads.items():
        noise = np.random.default_rng([zlib.crc32(name.encode()), seed]).standard_normal(out[name].shape)
        drawn = base * np.exp(spread * noise) if base else spread * noise
        out[name] = __import__('jax').numpy.asarray(drawn.astype(out[name].dtype))
    for name, factor in factors.items():
        out[name] = (out[name] * factor).astype(out[name].dtype)
    return out
```

```python
import math
from contextlib import ExitStack

import concourse.bass as bass
from concourse import mybir

F32 = mybir.dt.float32
I32 = mybir.dt.int32
U32 = mybir.dt.uint32
ALU = mybir.AluOpType
ACT = mybir.ActivationFunctionType
AXX = mybir.AxisListType.X

D = 1024
T = 128
SEQ = 512
NB = SEQ // T
DEPTH = 2
KT = D // 128
EPS = 1e-6
IN_W = 1732
AH, AHD, RANK = 8, 64, 128
IH = 4
TOPK = 128
PH, PK, NKEY = 8, 16, 128
HK = PH * PK
NEXP = NKEY * NKEY
NR = 8
GB = 4
NBAT = HK // GB
NEG = -1e30
GONE = -3e38
GELU_A, GELU_S = 0.044715, math.sqrt(2.0 / math.pi)
C_V, C_Q, C_CKV, C_QI, C_KI, C_WI = 512, 768, 1280, 1408, 1664, 1728
GROUPS = [(0, 512), (512, 512), (1024, 512), (1536, IN_W - 1536)]
SHIFT1, SCALE1, GATE1, SHIFT2, SCALE2, GATE2 = range(6)

NAMES = """x_in ss1 h_ready hT_ps hT_sb proj_ps proj_sb ki_cached bu_ps bu_used prods y_ps glu_in glu_th
yg_ready z_ps z_th vn_ready ckvn_ready g_ps mix_ready ckvT_ps ckv_cached sc_ps relu_sb qa_ps qa_sb
lg_ps lg_used nmax exp_done p_ready pt_ps pt_sb o_ps o_sb yc_ps yc_sb out_ps x1_ready ss2 h2_ready
h2T_ps h2T_sb pq_ps pq_sb s_ps top_ready gexp routed chain act_pre act_th w_ready diag_ready dots
mixed xn_ready x_stored x1_loaded x1_saved cc_exp crep_ready e_ready e_ps mod_ps mod_added params c_loaded w_l0 w_l1
gain_in state_re debug""".split()


def build(nc, A, out, debug=None):
    ctx = ExitStack()
    with ctx:
        def sb(name, cols, dt=F32, rows=128):
            return ctx.enter_context(nc.sbuf_tensor(name, [rows, cols], dt))

        def ps(name, cols):
            return ctx.enter_context(nc.psum_tensor(name, [128, cols], F32))

        ringU = [sb(f"ringU{i}", D) for i in range(NR)]
        ringV = [sb(f"ringV{i}", D) for i in range(NR)]
        wring = [sb(f"wring{i}", KT * 512) for i in range(2)]
        modb = sb("modb", 6 * D)
        wk = sb("wk", 4 * D)
        xs, hh, hT = sb("xs", D), sb("hh", D), sb("hT", D)
        mixT = sb("mixT", D)
        pr = sb("pr", 3 * 512 + 260)
        h2g, g2g = sb("h2g", D), sb("g2g", D)
        cosT, sinT = sb("cosT", D), sb("sinT", D)
        BBre, BBim = sb("BBre", 256), sb("BBim", 256)
        CCre, nCre, nCim = sb("CCre", 256), sb("nCre", 256), sb("nCim", 256)
        wglu, wuk, wuv, wsT = sb("wglu", 512), sb("wuk", 512), sb("wuv", 512), sb("wsT", 512)
        kT, kvg, bsp = sb("kT", 128), sb("kvg", 128), sb("bsp", 512, rows=1)
        ckv_all, ckvT_all, kiT_all = sb("ckv_all", 512), sb("ckvT_all", 512), sb("kiT_all", 512)
        nd0 = sb("nd0", 512)
        ident = sb("ident", 128)
        diag = sb("diag", GB * 128)
        ones = sb("ones", 64, rows=1)
        gate_w, gate_g = sb("gate_w", HK), sb("gate_g", HK)
        idx_w, idx_g = sb("idx_w", HK, U32), sb("idx_g", HK, U32)
        val, vix = sb("val", 256), sb("vix", 256, U32)
        cv, cpos = sb("cv", HK), sb("cpos", HK, U32)
        m8 = sb("m8", 8)
        sm = pr[:, 0:40 * 8]
        iota16 = sb("iota16", 16)
        cols = sb("cols", 64)
        it = sb("it", 16, I32)
        state = sb("state", 16)
        abat, atmp = sb("abat", 2 * GB), sb("atmp", 2 * GB)
        wbat = sb("wbat", 2 * GB)
        py = ps("py", D)
        pj = [ps("pj0", 512), ps("pj1", 512)]
        pw = ps("pw", 4 * 512)
        x_mid = nc.dram_tensor("x_mid", [SEQ, D], F32, kind="Internal").ap()
        x_mix = nc.dram_tensor("x_mix", [SEQ, D], F32, kind="Internal").ap()
        ux = A["peer_u"].rearrange("l e d -> (l e) d")
        vx = A["peer_v"].rearrange("l e d -> (l e) d")

        def col(i, n=1):
            return cols[:, i:i + n]
        SS1, RS1, SS2, RS2, B128, LIMP, PCOL, HALF, ODD = range(9)
        V5, R5, MU, DEN, NM, RD, WSC, DSK, BGH, CACT, EVEN = 9, 14, 19, 23, 31, 39, 47, 51, 53, 55, 63

        S = {n: ctx.enter_context(nc.semaphore(n)) for n in NAMES}
        nums = sorted(s.num for s in S.values())
        assert nums == list(range(nums[0], nums[0] + len(nums)))
        arrive = ctx.enter_context(nc.semaphore("arrive"))
        go = {e: ctx.enter_context(nc.semaphore("go_" + e)) for e in ("pool", "act", "pe", "dve")}
        landU = [ctx.enter_context(nc.semaphore(f"landU{i}")) for i in range(NR)]
        landV = [ctx.enter_context(nc.semaphore(f"landV{i}")) for i in range(NR)]
        consts = ctx.enter_context(nc.semaphore("consts"))
        LAND = 16 * HK // NR
        NPAR = 35

        def meet(eng, name):
            eng.drain().then_inc(arrive, 1)
            eng.wait_ge(go[name], 1)
            eng.sem_inc(go[name], -1)

        def legs(eng, leg):
            if debug:
                leg(0, 0, True, None, 0)
                if debug == "two":
                    leg(0, 1, True, None, 0)
                return
            leg(0, 0, True, None, 0)
            with eng.Fori(1, NB) as b:
                leg(0, b, True, (0, b - 1), (b - 1) * LAND)
            leg(1, 0, True, (0, NB - 1), (NB - 1) * LAND)
            with eng.Fori(1, NB) as b:
                leg(1, b, True, (1, b - 1), (b + (NB - 1)) * LAND)
            leg(1, 0, False, (1, NB - 1), (2 * NB - 1) * LAND)

        block = ctx.enter_context(nc.Block())

        def is_first(b):
            return isinstance(b, int) and b == 0

        @block.gpsimd
        def _(pool):
            pool.memset(ident[:, :], 0.0).then_inc(consts, 1)
            pool.memset(ones[:, :], 1.0).then_inc(consts, 1)
            pool.memset(ckv_all[:, :], 0.0).then_inc(consts, 1)
            pool.memset(ckvT_all[:, :], 0.0).then_inc(consts, 1)
            pool.memset(kiT_all[:, :], 0.0).then_inc(consts, 1)
            pool.iota(wk[:, 0:512].bitcast(I32), pattern=[[1, 512]], base=0, channel_multiplier=-1).then_inc(consts, 1)
            pool.iota(it[:, 0:1], pattern=[[0, 1]], base=0, channel_multiplier=1).then_inc(consts, 1)
            pool.iota(wk[:, 512:528].bitcast(I32), pattern=[[1, 16]], base=0, channel_multiplier=0).then_inc(consts, 1)
            pool.wait_ge(consts, 8)
            pool.affine_select(out=ident[:, :], in_=ident[:, :], compare_op=ALU.not_equal, fill=1.0,
                               base=0, pattern=[[-1, 128]], channel_multiplier=1).then_inc(consts, 1)

            def leg(l, b, mixers, g, before):
                if g is not None:
                    def rows(ring, land, src, j, freed):
                        for k in range(j * GB, (j + 1) * GB):
                            if k >= NR:
                                pool.wait_ge(freed, k - NR + 1)
                            pool.indirect_dma_start(
                                out=ring[k % NR][:, :], out_offset=None, in_=src,
                                in_offset=bass.IndirectOffsetOnAxis(ap=idx_g[:, k:k + 1], axis=0),
                            ).then_inc(land[k % NR], 16)
                    rows(ringU, landU, ux, 0, S["dots"])
                    for j in range(NBAT):
                        if j + 1 < NBAT:
                            rows(ringU, landU, ux, j + 1, S["dots"])
                        rows(ringV, landV, vx, j, S["mixed"])
                meet(pool, "pool")
            legs(pool, leg)

        @block.scalar
        def _(a):

            def leg(l, b, mixers, g, before):
                done = [0]

                def gathered(n):
                    if g is None:
                        return
                    while done[0] < n:
                        j = done[0]
                        if j < NBAT:
                            a.wait_ge(S["act_pre"], j + 1)
                            a.activation(atmp[:, (j % 2) * GB:(j % 2 + 1) * GB], atmp[:, (j % 2) * GB:(j % 2 + 1) * GB],
                                         ACT.Tanh, scale=GELU_S).then_inc(S["act_th"], 1)
                        if j >= 1:
                            a.wait_ge(S["w_ready"], j)
                            for k in range((j - 1) * GB, j * GB):
                                if k >= GB:
                                    a.wait_ge(S["mixed"], k - GB + 1)
                                a.activation(diag[:, (k % GB) * 128:(k % GB + 1) * 128], ident[:, :], ACT.Copy,
                                             scale=wbat[:, k % (2 * GB):k % (2 * GB) + 1]).then_inc(S["diag_ready"], 1)
                        done[0] += 1

                def copy(dst, src, sem):
                    a.activation(dst, src, ACT.Copy).then_inc(S[sem], 1)

                if mixers:
                    if is_first(b):
                        a.wait_ge(S["c_loaded"], 16)
                        a.activation(cols[:, EVEN - 8:EVEN], sm[:, 312:320], ACT.Exp, scale=-1.0).then_inc(S["cc_exp"], 1)
                    a.wait_ge(S["x_in"], 16)
                    if is_first(b):
                        gathered(2)
                        a.wait_ge(S["mod_added"], 24)
                    a.activation(hh[:, :], xs[:, :], ACT.Square, accum_out=col(SS1)).then_inc(S["ss1"], 1)
                    gathered(3)
                    for n in range(2):
                        a.wait_ge(S["hT_ps"], n + 1)
                        copy(hT[:, n * 512:(n + 1) * 512], pj[n][:, :], "hT_sb")
                    for n in range(4):
                        a.wait_ge(S["proj_ps"], n + 1)
                        wide = 512 if n < 3 else 260
                        copy(pr[:, n * 512:n * 512 + wide], pj[n % 2][:, 0:wide], "proj_sb")
                        if n < 3:
                            gathered(4 + n)
                    copy(kiT_all[:, bass.ds(b * T, T)], pj[1][:, 128:256], "ki_cached")
                    gathered(8)
                    a.wait_ge(S["ckvT_ps"], 1)
                    copy(ckvT_all[:, bass.ds(b * T, T)], pj[1][:, 256:384], "ckv_cached")
                    copy(ckv_all[:, bass.ds(b * T, T)], wk[:, 1664:1792], "ckv_cached")
                    a.wait_ge(S["glu_in"], 1)
                    a.activation(wk[:, 256:512], wk[:, 256:512], ACT.Tanh, scale=GELU_S).then_inc(S["glu_th"], 1)
                    gathered(9)
                    a.wait_ge(S["z_ps"], 1)
                    for j in range(2):
                        a.activation(wk[:, 512 + j * 128:640 + j * 128], pj[0][:, 256 + j * 128:384 + j * 128], ACT.Tanh,
                                     scale=0.5, bias=col(BGH + j)).then_inc(S["z_th"], 1)
                    for h in range(IH):
                        a.wait_ge(S["sc_ps"], h + 1)
                        a.activation(wk[:, 2048 + h * 512:2560 + h * 512], pw[:, h * 512:(h + 1) * 512],
                                     ACT.Relu).then_inc(S["relu_sb"], 1)
                    for n in range(2):
                        a.wait_ge(S["qa_ps"], n + 1)
                        a.activation(hh[:, n * 512:(n + 1) * 512], pj[n][:, :], ACT.Copy,
                                     scale=AHD ** -0.5).then_inc(S["qa_sb"], 1)
                    gathered(16)

                    def evac_p(h):
                        a.wait_ge(S["pt_ps"], h + 1)
                        if h >= 2:
                            a.wait_ge(S["o_ps"], h - 1)
                        copy(hT[:, (h % 2) * 512:(h % 2 + 1) * 512], pj[h % 2][:, :], "pt_sb")
                        if h in (3, 7):
                            a.wait_ge(S["o_ps"], h + 1)
                            if h == 3:
                                a.wait_ge(S["mix_ready"], 2)
                            copy(pr[:, (h // 4) * 512:(h // 4 + 1) * 512], pw[:, 1024:1536], "o_sb")
                    for h in range(AH):
                        a.wait_ge(S["nmax"], h + 1)
                        if h >= 2:
                            a.wait_ge(S["pt_ps"], h - 1)
                        a.activation(wk[:, 3072 + (h % 2) * 512:3584 + (h % 2) * 512], wk[:, 2048 + (h % 2) * 512:2560 + (h % 2) * 512],
                                     ACT.Exp, bias=col(NM + h), accum_out=col(DEN + h)).then_inc(S["exp_done"], 1)
                        if h >= 1:
                            evac_p(h - 1)
                        gathered(16 + h // 2)
                    evac_p(AH - 1)
                    a.wait_ge(S["yc_ps"], 1)
                    copy(mixT[:, 512:1024], pw[:, 1536:2048], "yc_sb")
                    gathered(20)
                    a.wait_ge(S["x1_ready"], 2)
                    gathered(21)
                    a.activation(wk[:, 1024:2048], xs[:, :], ACT.Square, accum_out=col(SS2)).then_inc(S["ss2"], 1)
                    gathered(23)
                    for n in range(2):
                        a.wait_ge(S["h2T_ps"], n + 1)
                        copy(hT[:, n * 512:(n + 1) * 512], pj[n][:, :], "h2T_sb")
                    for n in range(2):
                        a.wait_ge(S["pq_ps"], n + 1)
                        copy(pr[:, n * 512:(n + 1) * 512], pj[n][:, :], "pq_sb")
                        if n == 0:
                            gathered(24)
                    gathered(29)
                    a.wait_ge(S["top_ready"], 1)
                    a.activation(gate_w[:, :], gate_w[:, :], ACT.Exp).then_inc(S["gexp"], 1)
                gathered(NBAT + 1)
                meet(a, "act")
            legs(a, leg)

        @block.tensor
        def _(t):
            t.wait_ge(consts, 9)

            def leg(l, b, mixers, g, before):
                done = [0]

                def gathered(n):
                    if g is None:
                        return
                    while done[0] < n:
                        j = done[0]
                        if j >= 1:
                            for k in range((j - 1) * GB, j * GB):
                                t.wait_ge(S["diag_ready"], k + 1)
                                t.wait_ge(landV[k % NR], before + 16 * (k // NR + 1))
                                for c in range(2):
                                    mm = t.matmul(py[:, c * 512:(c + 1) * 512], diag[:, (k % GB) * 128:(k % GB + 1) * 128],
                                                  ringV[k % NR][:, c * 512:(c + 1) * 512], start=k == 0, stop=k == HK - 1)
                                mm.then_inc(S["mixed"], 1)
                        done[0] += 1

                def turn(dst, src, last=None):
                    m = t.transpose(dst, src, ident[:, :])
                    if last:
                        m.then_inc(S[last], 1)

                wn = [0]

                def weights():
                    n = wn[0]
                    wn[0] += 1
                    t.wait_ge(S[f"w_l{n % 2}"], 16 * (n // 2 + 1))
                    return wring[n % 2]

                if mixers:
                    if is_first(b):
                        t.wait_ge(S["e_ready"], 1)
                        for i in range(2):
                            turn(pw[:, i * 128:(i + 1) * 128], wk[:, 512 + i * 128:640 + i * 128])
                            turn(pw[:, 256 + i * 128:384 + i * 128], wk[:, 768 + i * 128:896 + i * 128])
                            turn(pw[:, 512 + i * 128:640 + i * 128], wk[:, 1280 + i * 128:1408 + i * 128])
                            turn(pw[:, 768 + i * 128:896 + i * 128], wk[:, 1536 + i * 128:1664 + i * 128])
                        for h in range(4):
                            turn(pw[:, 1024 + h * 128:1152 + h * 128], wk[:, 2048 + h * 128:2176 + h * 128])
                        turn(pw[:, 1536:1664], wk[:, 1792:1920], "e_ps")
                        t.wait_ge(S["crep_ready"], 1)
                        for n in range(12):
                            wt = weights()
                            if n >= 2:
                                t.wait_ge(S["mod_added"], n - 1)
                            for k in range(KT):
                                mm = t.matmul(pj[n % 2][:, :], mixT[:, k * 128:(k + 1) * 128], wt[:, k * 512:(k + 1) * 512],
                                              start=k == 0, stop=k == KT - 1)
                            mm.then_inc(S["mod_ps"], 1)
                            gathered(n // 4)
                    gathered(2)
                    t.wait_ge(S["h_ready"], 1)
                    for k in range(KT):
                        turn(pj[k // 4][:, (k % 4) * 128:(k % 4 + 1) * 128], hh[:, k * 128:(k + 1) * 128],
                             "hT_ps" if k % 4 == 3 else None)
                    t.wait_ge(S["hT_sb"], 2)

                    def across(dst, wt, gc, c0, width, last=None):
                        for k in range(KT):
                            mm = t.matmul(dst, wt[:, k * gc + c0:k * gc + c0 + width], hT[:, k * 128:(k + 1) * 128],
                                          start=k == 0, stop=k == KT - 1)
                        return mm

                    def along(dst, wt, gc, c0, width):
                        for k in range(KT):
                            mm = t.matmul(dst, hT[:, k * 128:(k + 1) * 128], wt[:, k * gc + c0:k * gc + c0 + width],
                                          start=k == 0, stop=k == KT - 1)
                        return mm

                    wt = weights()
                    for f in range(4):
                        mm = across(pj[0][:, f * 128:(f + 1) * 128], wt, 512, f * 128, 128)
                    mm.then_inc(S["proj_ps"], 1)
                    gathered(3)
                    wt = weights()
                    along(pj[1][:, 0:256], wt, 512, 0, 256)
                    for f in range(2):
                        mm = across(pj[1][:, 256 + f * 128:384 + f * 128], wt, 512, 256 + f * 128, 128)
                    mm.then_inc(S["proj_ps"], 1)
                    t.wait_ge(S["proj_sb"], 1)
                    for ri, BB in enumerate((BBre, BBim)):
                        for j in range(2):
                            for q in range(4):
                                mm = t.matmul(pw[:, q * 512 + ri * 256 + j * 128:q * 512 + ri * 256 + (j + 1) * 128],
                                              BB[32 * q:32 * q + 32, j * 128:(j + 1) * 128],
                                              pr[32 * q:32 * q + 32, j * 128:(j + 1) * 128], start=True, stop=True)
                    mm.then_inc(S["bu_ps"], 1)
                    gathered(4)
                    wt = weights()
                    for f in range(2):
                        across(pj[0][:, f * 128:(f + 1) * 128], wt, 512, f * 128, 128)
                    along(pj[0][:, 256:384], wt, 512, 256, 128)
                    across(pj[0][:, 384:512], wt, 512, 384, 128).then_inc(S["proj_ps"], 1)
                    gathered(5)
                    wt = weights()
                    gc = GROUPS[3][1]
                    t.wait_ge(S["proj_sb"], 2)
                    across(pj[1][:, 0:128], wt, gc, 0, 128)
                    across(pj[1][0:64, 128:256], wt, gc, 128, 64)
                    across(pj[1][64:128, 128:256], wt, gc, 128, 64)
                    along(pj[1][:, 256:260], wt, gc, 192, 4).then_inc(S["proj_ps"], 1)
                    gathered(6)
                    t.wait_ge(S["prods"], 1)
                    t.wait_ge(S["proj_sb"], 3)
                    for j in range(2):
                        for q in range(4):
                            m = q * 2 + j
                            dst = pj[0][32 * q:32 * q + 32, j * 128:(j + 1) * 128]
                            cs = slice(j * 128 + 32 * q, j * 128 + 32 * q + 32)
                            for i, (C, at) in enumerate(((CCre, 0), (nCre, 2048), (nCim, 1024), (nCim, 3072))):
                                mm = t.matmul(dst, C[:, cs], wk[:, at + m * 128:at + (m + 1) * 128], start=i == 0, stop=i == 3)
                    mm.then_inc(S["y_ps"], 1)
                    gathered(7)
                    t.wait_ge(S["vn_ready"], 1)
                    t.wait_ge(S["ki_cached"], 1)
                    for h in range(4):
                        dst = pj[1][64 * (h % 2):64 * (h % 2) + 64, (h // 2) * 128:(h // 2 + 1) * 128]
                        t.matmul(dst, wk[:, 1024 + h * 64:1088 + h * 64], wsT[:, h * 128:(h + 1) * 128], start=True, stop=False)
                        mm = t.matmul(dst, ones[0:1, 0:64], bsp[0:1, h * 128:(h + 1) * 128], start=False, stop=True)
                    mm.then_inc(S["g_ps"], 1)
                    t.wait_ge(S["ckvn_ready"], 1)
                    t.wait_ge(S["mix_ready"], 1)
                    turn(pj[1][:, 256:384], wk[:, 1664:1792], "ckvT_ps")
                    gathered(8)
                    t.wait_ge(S["yg_ready"], 1)
                    for jo in range(2):
                        for ji in range(2):
                            mm = t.matmul(pj[0][:, 256 + jo * 128:384 + jo * 128],
                                          wglu[:, ji * 256 + jo * 128:ji * 256 + (jo + 1) * 128],
                                          wk[:, ji * 128:(ji + 1) * 128], start=ji == 0, stop=ji == 1)
                    mm.then_inc(S["z_ps"], 1)
                    t.wait_ge(S["bu_used"], 1)
                    for h in range(IH):
                        lo = 64 * (h % 2)
                        at = 1408 if h < 2 else 1536
                        t.matmul(pw[:, h * 512:(h + 1) * 512], pr[lo:lo + 64, at:at + 128], kiT_all[lo:lo + 64, :],
                                 start=True, stop=True).then_inc(S["sc_ps"], 1)
                    t.wait_ge(S["z_th"], 2)
                    t.wait_ge(S["ckv_cached"], 2)
                    for n in range(2):
                        for i in range(4):
                            at = 768 + i * 128 if i < 2 else 1024 + (i - 2) * 128
                            mm = t.matmul(pj[n][:, i * 128:(i + 1) * 128], wuk[64 * n:64 * n + 64, i * 128:(i + 1) * 128],
                                          pr[64 * n:64 * n + 64, at:at + 128], start=True, stop=True)
                        mm.then_inc(S["qa_ps"], 1)
                    gathered(15)
                    t.wait_ge(S["relu_sb"], 4)
                    t.wait_ge(S["qa_sb"], 2)

                    def logits(h):
                        if h >= 2:
                            t.wait_ge(S["lg_used"], h - 1)
                        q = hh[:, (h % 2) * 512 + (h // 2) * 128:(h % 2) * 512 + (h // 2 + 1) * 128]
                        t.matmul(pw[:, (h % 2) * 512:(h % 2 + 1) * 512], q, ckvT_all[:, :],
                                 start=True, stop=True).then_inc(S["lg_ps"], 1)

                    def values(h):
                        t.wait_ge(S["p_ready"], h + 1)
                        if h >= 2:
                            t.wait_ge(S["pt_sb"], h - 1)
                        for s in range(4):
                            turn(pj[h % 2][:, s * 128:(s + 1) * 128], wk[:, 3072 + (h % 2) * 512 + s * 128:3200 + (h % 2) * 512 + s * 128],
                                 "pt_ps" if s == 3 else None)
                        t.wait_ge(S["pt_sb"], h + 1)
                        if h == 4:
                            t.wait_ge(S["o_sb"], 1)
                        for s in range(4):
                            mm = t.matmul(pw[:, 1024 + (h % 4) * 128:1152 + (h % 4) * 128], ckv_all[:, s * 128:(s + 1) * 128],
                                          hT[:, (h % 2) * 512 + s * 128:(h % 2) * 512 + (s + 1) * 128], start=s == 0, stop=s == 3)
                        mm.then_inc(S["o_ps"], 1)
                    for h in range(AH):
                        logits(h)
                        if h >= 1:
                            values(h - 1)
                        gathered(15 + h // 2)
                    values(AH - 1)
                    t.wait_ge(S["o_sb"], 2)
                    for h in range(AH):
                        mm = t.matmul(pw[64 * (h % 2):64 * (h % 2) + 64, 1536 + (h // 2) * 128:1664 + (h // 2) * 128],
                                      wuv[:, h * 64:(h + 1) * 64], pr[:, h * 128:(h + 1) * 128], start=True, stop=True)
                    mm.then_inc(S["yc_ps"], 1)
                    gathered(19)
                    t.wait_ge(S["yc_sb"], 1)
                    for n in range(2):
                        wt = weights()
                        for k in range(KT):
                            mm = t.matmul(pj[n][:, :], mixT[:, k * 128:(k + 1) * 128], wt[:, k * 512:(k + 1) * 512],
                                          start=k == 0, stop=k == KT - 1)
                        mm.then_inc(S["out_ps"], 1)
                    gathered(22)
                    t.wait_ge(S["h2_ready"], 1)
                    for k in range(KT):
                        turn(pj[k // 4][:, (k % 4) * 128:(k % 4 + 1) * 128], hh[:, k * 128:(k + 1) * 128],
                             "h2T_ps" if k % 4 == 3 else None)
                    t.wait_ge(S["h2T_sb"], 2)
                    for n in range(2):
                        wt = weights()
                        for f in range(4):
                            mm = across(pj[n][:, f * 128:(f + 1) * 128], wt, 512, f * 128, 128)
                        mm.then_inc(S["pq_ps"], 1)
                        if n == 0:
                            gathered(23)
                    t.wait_ge(S["pq_sb"], 2)
                    for half in range(2):
                        for f in range(PH):
                            mm = t.matmul(pw[:, (half * 8 + f) * 128:(half * 8 + f + 1) * 128], pr[64 * half:64 * half + 64, f * 128:(f + 1) * 128],
                                          kT[64 * half:64 * half + 64, :], start=True, stop=True)
                    mm.then_inc(S["s_ps"], 1)
                    gathered(28)
                gathered(NBAT + 1)
                meet(t, "pe")
            legs(t, leg)

        @block.vector
        def _(v):
            v.wait_ge(consts, 9)
            v.tensor_copy(nd0[:, :], wk[:, 0:512].bitcast(I32)).then_inc(consts, 1)
            v.tensor_copy(col(PCOL), it[:, 0:1]).then_inc(consts, 1)
            v.tensor_copy(iota16[:, :], wk[:, 512:528].bitcast(I32)).then_inc(consts, 1)
            v.tensor_scalar(it[:, 1:2], it[:, 0:1], 4, 1, ALU.logical_shift_right, ALU.bitwise_and).then_inc(consts, 1)
            v.wait_ge(consts, 13)
            v.tensor_scalar(col(HALF), col(PCOL), 64.0, None, ALU.is_ge).then_inc(consts, 1)
            v.tensor_copy(col(ODD), it[:, 1:2]).then_inc(consts, 1)
            v.wait_ge(consts, 15)
            v.tensor_scalar(col(EVEN), col(ODD), -1.0, 1.0, ALU.mult, ALU.add).then_inc(consts, 1)
            v.wait_ge(consts, 16)

            def leg(l, b, mixers, g, before):
                done, chained = [0], [0]

                def link(ins):
                    chained[0] += 1
                    ins.then_inc(S["chain"], 1)
                    v.wait_ge(S["chain"], chained[0])

                def note(ins):
                    chained[0] += 1
                    ins.then_inc(S["chain"], 1)

                def settled():
                    v.wait_ge(S["chain"], chained[0])

                def weigh(j):
                    v.wait_ge(S["act_th"], j + 1)
                    s = slice((j % 2) * GB, (j % 2 + 1) * GB)
                    link(v.scalar_tensor_tensor(wbat[:, s], atmp[:, s], 1.0, abat[:, s], ALU.add, ALU.mult))
                    v.tensor_tensor(wbat[:, s], wbat[:, s], gate_g[:, j * GB:(j + 1) * GB], ALU.mult).then_inc(S["w_ready"], 1)

                def gathered(n):
                    if g is None:
                        return
                    while done[0] < n:
                        j = done[0]
                        if j < NBAT:
                            s = slice((j % 2) * GB, (j % 2 + 1) * GB)
                            for k in range(j * GB, (j + 1) * GB):
                                v.wait_ge(landU[k % NR], before + 16 * (k // NR + 1))
                                c = k % (2 * GB)
                                v.tensor_tensor_reduce(out=ringU[k % NR][:, :], in0=ringU[k % NR][:, :], in1=h2g[:, :],
                                                       scale=1.0, scalar=0.0, op0=ALU.mult, op1=ALU.add,
                                                       accum_out=abat[:, c:c + 1]).then_inc(S["dots"], 1)
                            v.wait_ge(S["dots"], (j + 1) * GB)
                            link(v.tensor_tensor(atmp[:, s], abat[:, s], abat[:, s], ALU.mult))
                            link(v.tensor_scalar(atmp[:, s], atmp[:, s], GELU_A, 1.0, ALU.mult, ALU.add))
                            v.tensor_tensor(atmp[:, s], atmp[:, s], abat[:, s], ALU.mult).then_inc(S["act_pre"], 1)
                        if j >= 1:
                            if j >= 3:
                                v.wait_ge(S["diag_ready"], (j - 2) * GB)
                            weigh(j - 1)
                        done[0] += 1

                def rsqrt(dst, src, bits):
                    tmp = bits.bitcast(F32)
                    link(v.tensor_scalar(bits, src.bitcast(I32), 1, None, ALU.logical_shift_right))
                    link(v.tensor_scalar(dst.bitcast(I32), bits, -1.0, float(0x5f3759df), ALU.mult, ALU.add))
                    for _ in range(3):
                        link(v.tensor_tensor(tmp, dst, dst, ALU.mult))
                        link(v.tensor_tensor(tmp, tmp, src, ALU.mult))
                        link(v.tensor_scalar(tmp, tmp, -0.5, 1.5, ALU.mult, ALU.add))
                        link(v.tensor_tensor(dst, dst, tmp, ALU.mult))

                def sm8(i):
                    return sm[:, i * 8:(i + 1) * 8]

                def exp8(dst, x, lo, hi):
                    n, r, p, q = sm8(24), sm8(25), sm8(26), sm8(27)
                    link(v.tensor_scalar(r, x, lo, hi, ALU.max, ALU.min))
                    link(v.tensor_scalar(n, r, 1.4426950408889634, None, ALU.mult))
                    link(v.tensor_scalar(n, n, 12582912.0, None, ALU.add))
                    link(v.tensor_scalar(n, n, 12582912.0, None, ALU.subtract))
                    link(v.scalar_tensor_tensor(r, n, -0.693359375, r, ALU.mult, ALU.add))
                    link(v.scalar_tensor_tensor(r, n, 2.12194440e-4, r, ALU.mult, ALU.add))
                    link(v.tensor_scalar(p, r, 1.0 / 5040, 1.0 / 720, ALU.mult, ALU.add))
                    for c in (1.0 / 120, 1.0 / 24, 1.0 / 6, 0.5, 1.0, 1.0):
                        link(v.tensor_tensor(p, p, r, ALU.mult))
                        link(v.tensor_scalar(p, p, c, None, ALU.add))
                    link(v.tensor_scalar(n, n, 127.0, None, ALU.add))
                    link(v.tensor_copy(q.bitcast(I32), n))
                    link(v.tensor_scalar(q.bitcast(I32), q.bitcast(I32), 23, None, ALU.logical_shift_left))
                    link(v.tensor_tensor(dst, p, q, ALU.mult))

                def parameters():
                    v.wait_ge(S["cc_exp"], 1)
                    e = cols[:, EVEN - 8:EVEN]
                    link(v.tensor_scalar(e, e, 1.0, None, ALU.add))
                    link(v.reciprocal(e, e))
                    link(v.tensor_tensor(e, e, sm[:, 312:320], ALU.mult))
                    v.tensor_copy(mixT[:, :].rearrange("p (k m) -> p k m", k=KT),
                                  e.unsqueeze(2).broadcast_to([128, KT, 128])).then_inc(S["crep_ready"], 1)
                    v.wait_ge(S["params"], 16 * NPAR)
                    are, aim, ldt = sm8(0), sm8(1), sm8(2)
                    dt, lre, mag = sm8(3), sm8(4), sm8(5)
                    exp8(dt, ldt, -87.0, 88.0)
                    exp8(lre, are, -87.0, 88.0)
                    link(v.tensor_scalar(lre, lre, -1.0, None, ALU.mult))
                    link(v.tensor_tensor(sm8(6), lre, dt, ALU.mult))
                    exp8(mag, sm8(6), -87.0, 88.0)
                    th, n, mq, r, r2 = sm8(7), sm8(8), sm8(9), sm8(10), sm8(11)
                    sn, cs, sq, cq = sm8(12), sm8(13), sm8(14), sm8(15)
                    link(v.tensor_tensor(th, aim, dt, ALU.mult))
                    link(v.tensor_scalar(n, th, 2.0 / math.pi, None, ALU.mult))
                    link(v.tensor_scalar(n, n, 12582912.0, None, ALU.add))
                    link(v.tensor_scalar(n, n, 12582912.0, None, ALU.subtract))
                    link(v.scalar_tensor_tensor(r, n, -1.5703125, th, ALU.mult, ALU.add))
                    link(v.scalar_tensor_tensor(r, n, -4.8375129699707031e-4, r, ALU.mult, ALU.add))
                    link(v.scalar_tensor_tensor(r, n, -7.5497899548918e-8, r, ALU.mult, ALU.add))
                    link(v.tensor_tensor(r2, r, r, ALU.mult))
                    link(v.tensor_scalar(sn, r2, 2.7557319e-6, -1.9841270e-4, ALU.mult, ALU.add))
                    for c in (8.3333333e-3, -0.16666667):
                        link(v.tensor_tensor(sn, sn, r2, ALU.mult))
                        link(v.tensor_scalar(sn, sn, c, None, ALU.add))
                    link(v.tensor_tensor(sn, sn, r2, ALU.mult))
                    link(v.scalar_tensor_tensor(sn, sn, 1.0, r, ALU.mult, ALU.mult))
                    link(v.tensor_tensor(sn, sn, r, ALU.add))
                    link(v.tensor_scalar(cs, r2, 2.4801587e-5, -1.3888889e-3, ALU.mult, ALU.add))
                    for c in (4.1666667e-2, -0.5, 1.0):
                        link(v.tensor_tensor(cs, cs, r2, ALU.mult))
                        link(v.tensor_scalar(cs, cs, c, None, ALU.add))
                    link(v.tensor_scalar(mq, n, 0.25, None, ALU.mult))
                    link(v.tensor_scalar(mq, mq, 12582912.0, None, ALU.add))
                    link(v.tensor_scalar(mq, mq, 12582912.0, None, ALU.subtract))
                    link(v.scalar_tensor_tensor(mq, mq, -4.0, n, ALU.mult, ALU.add))
                    link(v.scalar_tensor_tensor(cq, mq, -1.0, mq, ALU.mult, ALU.min))
                    link(v.tensor_scalar(sq, cq, 2.0, None, ALU.add))
                    link(v.tensor_tensor(sq, sq, mq, ALU.mult))
                    link(v.tensor_scalar(cq, cq, 1.0, None, ALU.add))
                    cr, ci, t1, t2 = sm8(16), sm8(17), sm8(18), sm8(19)
                    link(v.tensor_tensor(t1, cq, cs, ALU.mult))
                    link(v.tensor_tensor(t2, sq, sn, ALU.mult))
                    link(v.tensor_tensor(cr, t1, t2, ALU.subtract))
                    link(v.tensor_tensor(t1, sq, cs, ALU.mult))
                    link(v.tensor_tensor(t2, cq, sn, ALU.mult))
                    link(v.tensor_tensor(ci, t1, t2, ALU.add))
                    C3 = cosT[:, :].rearrange("p (m t) -> p m t", m=8)
                    S3 = sinT[:, :].rearrange("p (m t) -> p m t", m=8)
                    T1 = wk[:, 2560:3072].rearrange("p (m t) -> p m t", m=8)
                    T2 = wk[:, 3072:3584].rearrange("p (m t) -> p m t", m=8)
                    link(v.tensor_copy(C3[:, :, 0:1], cr.unsqueeze(2)))
                    link(v.tensor_copy(S3[:, :, 0:1], ci.unsqueeze(2)))
                    n = 1
                    while n < T:
                        cb = C3[:, :, n - 1:n].broadcast_to([128, 8, n])
                        sb_ = S3[:, :, n - 1:n].broadcast_to([128, 8, n])
                        link(v.tensor_tensor(T1[:, :, 0:n], C3[:, :, 0:n], cb, ALU.mult))
                        link(v.tensor_tensor(T2[:, :, 0:n], S3[:, :, 0:n], sb_, ALU.mult))
                        link(v.tensor_tensor(C3[:, :, n:2 * n], T1[:, :, 0:n], T2[:, :, 0:n], ALU.subtract))
                        link(v.tensor_tensor(T1[:, :, 0:n], C3[:, :, 0:n], sb_, ALU.mult))
                        link(v.tensor_tensor(T2[:, :, 0:n], S3[:, :, 0:n], cb, ALU.mult))
                        link(v.tensor_tensor(S3[:, :, n:2 * n], T1[:, :, 0:n], T2[:, :, 0:n], ALU.add))
                        n *= 2
                    pp, qq, den, fre, fim = sm8(20), sm8(21), sm8(22), sm8(23), sm8(28)
                    link(v.tensor_tensor(pp, mag, cr, ALU.mult))
                    link(v.tensor_scalar(pp, pp, 1.0, None, ALU.subtract))
                    link(v.tensor_tensor(qq, mag, ci, ALU.mult))
                    link(v.tensor_tensor(t1, lre, lre, ALU.mult))
                    link(v.tensor_tensor(t2, aim, aim, ALU.mult))
                    link(v.tensor_tensor(den, t1, t2, ALU.add))
                    link(v.reciprocal(den, den))
                    link(v.tensor_tensor(t1, pp, lre, ALU.mult))
                    link(v.tensor_tensor(t2, qq, aim, ALU.mult))
                    link(v.tensor_tensor(fre, t1, t2, ALU.add))
                    link(v.tensor_tensor(fre, fre, den, ALU.mult))
                    link(v.tensor_tensor(t1, qq, lre, ALU.mult))
                    link(v.tensor_tensor(t2, pp, aim, ALU.mult))
                    link(v.tensor_tensor(fim, t1, t2, ALU.subtract))
                    link(v.tensor_tensor(fim, fim, den, ALU.mult))

                    def by8(x):
                        return x.unsqueeze(2).broadcast_to([128, 8, 16])

                    def v3(x):
                        return x.rearrange("p (m h) -> p m h", m=8)
                    br, bi = v3(wk[:, 0:128]), v3(wk[:, 128:256])
                    bbr, bbi, tb = v3(wk[:, 256:384]), v3(wk[:, 384:512]), v3(wk[:, 1920:2048])
                    link(v.tensor_tensor(bbr, br, by8(fre), ALU.mult))
                    link(v.tensor_tensor(tb, bi, by8(fim), ALU.mult))
                    link(v.tensor_tensor(bbr, bbr, tb, ALU.subtract))
                    link(v.tensor_tensor(bbi, bi, by8(fre), ALU.mult))
                    link(v.tensor_tensor(tb, br, by8(fim), ALU.mult))
                    link(v.tensor_tensor(bbi, bbi, tb, ALU.add))
                    link(v.memset(wk[:, 512:1024], 0.0))
                    for src, at in ((bbr, 512), (bbi, 768)):
                        e5 = wk[:, at:at + 256].rearrange("p (j q g h) -> p j q g h", j=2, q=4, g=2)
                        s5 = src.rearrange("p (q j) h -> p j q h", j=2)
                        for gg in range(2):
                            lo = 64 * gg
                            note(v.tensor_copy(e5[lo:lo + 64, :, :, gg, :], s5[lo:lo + 64]))
                    for at, to in ((1024, 1280), (1152, 1536)):
                        for gg, msk in ((0, EVEN), (1, ODD)):
                            c4 = wk[:, to:to + 256].rearrange("p (j g n) -> p j g n", j=2, g=2)[:, :, gg, :]
                            s4 = wk[:, at:at + 128].rearrange("p (j n) -> p j n", j=2)
                            note(v.tensor_scalar(c4, s4, col(msk), None, ALU.mult))
                    settled()
                    v.tensor_copy(m8[:, :], mag).then_inc(S["e_ready"], 1)
                    v.wait_ge(S["e_ps"], 1)
                    note(v.tensor_copy(BBre[:, :], pw[:, 0:256]))
                    note(v.tensor_copy(BBim[:, :], pw[:, 256:512]))
                    note(v.tensor_copy(CCre[:, :], pw[:, 512:768]))
                    note(v.tensor_scalar(nCre[:, :], pw[:, 512:768], -1.0, None, ALU.mult))
                    note(v.tensor_scalar(nCim[:, :], pw[:, 768:1024], -1.0, None, ALU.mult))
                    note(v.tensor_copy(wsT[:, :], pw[:, 1024:1536]))
                    note(v.tensor_copy(kT[:, :], pw[:, 1536:1664]))
                    settled()
                    link(v.memset(wsT[64:128, :].rearrange("p (h t) -> p h t", h=4)[:, :, 0:64], 0.0))
                    link(v.tensor_scalar(cols[:, BGH:BGH + 2], cols[:, BGH:BGH + 2], 0.5, None, ALU.mult))
                    link(v.memset(state[:, :], 0.0))
                    link(v.memset(col(B128), 0.0))
                    link(v.tensor_scalar(col(LIMP), col(HALF), 64.0, 64.0, ALU.mult, ALU.add))
                    link(v.tensor_tensor(col(LIMP), col(LIMP), col(PCOL), ALU.subtract))
                    gathered(1)
                    for n in range(12):
                        v.wait_ge(S["mod_ps"], n + 1)
                        v.tensor_tensor(modb[:, n * 512:(n + 1) * 512], modb[:, n * 512:(n + 1) * 512], pj[n % 2][:, :],
                                        ALU.add).then_inc(S["mod_added"], 1)
                        gathered(n // 4)
                    v.wait_ge(S["mod_added"], 12)
                    for i, gain in ((SCALE1, hh), (SCALE2, hT)):
                        m = modb[:, i * D:(i + 1) * D]
                        v.scalar_tensor_tensor(m, m, 1.0, gain[:, :], ALU.add, ALU.mult).then_inc(S["mod_added"], 6)
                    v.wait_ge(S["mod_added"], 24)

                def mod(i, c0=0, n=D):
                    return modb[:, i * D + c0:i * D + c0 + n]

                def normed(ss, rs, scale, shift, ready):
                    link(v.tensor_scalar(col(ss), col(ss), 1.0 / D, EPS, ALU.mult, ALU.add))
                    rsqrt(col(rs), col(ss), it[:, 2:3])
                    link(v.scalar_tensor_tensor(hh[:, :], xs[:, :], col(rs), mod(scale), ALU.mult, ALU.mult))
                    v.tensor_tensor(hh[:, :], hh[:, :], mod(shift), ALU.add).then_inc(S[ready], 1)

                def mixer():
                    if is_first(b):
                        parameters()
                    else:
                        link(v.tensor_scalar(col(B128), col(B128), 128.0, None, ALU.add))
                        link(v.tensor_scalar(col(LIMP), col(LIMP), 128.0, None, ALU.add))
                    gathered(1)
                    v.wait_ge(S["ss1"], 1)
                    normed(SS1, RS1, SCALE1, SHIFT1, "h_ready")
                    gathered(5)
                    v.wait_ge(S["bu_ps"], 1)
                    pq = pw[:, :].rearrange("p (q r x) -> p q r x", q=4, r=2)
                    bre, bim = pq[:, :, 0, :], pq[:, :, 1, :]

                    def q4(x):
                        return x.rearrange("p (q x) -> p q x", q=4)
                    t1, t2, t3, t4 = (wk[:, i * D:(i + 1) * D] for i in range(4))
                    cosq, sinq = q4(cosT[:, :]), q4(sinT[:, :])
                    note(v.tensor_tensor(q4(t1), bre, cosq, ALU.mult))
                    note(v.tensor_tensor(q4(t2), bim, sinq, ALU.mult))
                    note(v.tensor_tensor(q4(t3), bim, cosq, ALU.mult))
                    settled()
                    v.tensor_tensor(q4(t4), bre, sinq, ALU.mult).then_inc(S["bu_used"], 1)
                    note(v.tensor_tensor(t1, t1, t2, ALU.add))
                    v.wait_ge(S["bu_used"], 1)
                    link(v.tensor_tensor(t3, t3, t4, ALU.subtract))
                    gathered(6)
                    for m in range(8):
                        ms = slice(m * 128, (m + 1) * 128)
                        mg = m8[:, m:m + 1].broadcast_to([128, 128])
                        note(v.tensor_tensor_scan(t2[:, ms], mg, t1[:, ms], state[:, m:m + 1], ALU.mult, ALU.add))
                        note(v.tensor_tensor_scan(t4[:, ms], mg, t3[:, ms], state[:, 8 + m:9 + m], ALU.mult, ALU.add))
                    settled()
                    gathered(7)
                    note(v.tensor_tensor(t1, t2, cosT[:, :], ALU.mult))
                    note(v.tensor_tensor(t3, t4, sinT[:, :], ALU.mult))
                    settled()
                    note(v.tensor_tensor(t2, t2, sinT[:, :], ALU.mult))
                    link(v.tensor_tensor(t4, t4, cosT[:, :], ALU.mult))

                    def last(x):
                        return x.rearrange("p (m t) -> p m t", m=8)[:, :, T - 1]
                    v.tensor_tensor(state[:, 0:8], last(t1), last(t3), ALU.subtract).then_inc(S["state_re"], 1)
                    v.tensor_tensor(state[:, 8:16], last(t2), last(t4), ALU.add).then_inc(S["prods"], 1)
                    v.wait_ge(S["y_ps"], 1)
                    v.wait_ge(S["proj_sb"], 3)
                    vb, vc, sq = pr[:, 512:768], wk[:, 1024:1280], wk[:, 1280:1536]

                    def h4(x):
                        return x.rearrange("p (h d) -> p h d", h=4)

                    def bc4(x):
                        return x.unsqueeze(2).broadcast_to([128, 4, 64])
                    link(v.tensor_reduce(col(MU, 4), h4(vb), AXX, ALU.add))
                    link(v.tensor_scalar(col(MU, 4), col(MU, 4), 1.0 / 64, None, ALU.mult))
                    link(v.tensor_tensor(h4(vc), h4(vb), bc4(col(MU, 4)), ALU.subtract))
                    link(v.tensor_tensor(sq, vc, vc, ALU.mult))
                    link(v.tensor_reduce(col(V5, 4), h4(sq), AXX, ALU.add))
                    ckv = pr[:, 1280:1408]
                    link(v.tensor_tensor_reduce(out=wk[:, 1536:1664], in0=ckv, in1=ckv, scale=1.0, scalar=0.0,
                                                op0=ALU.mult, op1=ALU.add, accum_out=col(V5 + 4)))
                    note(v.tensor_scalar(col(V5, 4), col(V5, 4), 1.0 / 64, EPS, ALU.mult, ALU.add))
                    link(v.tensor_scalar(col(V5 + 4), col(V5 + 4), 1.0 / RANK, EPS, ALU.mult, ALU.add))
                    rsqrt(col(R5, 5), col(V5, 5), it[:, 3:8])
                    v.tensor_tensor(h4(vc), h4(vc), bc4(col(R5, 4)), ALU.mult).then_inc(S["vn_ready"], 1)
                    v.scalar_tensor_tensor(wk[:, 1664:1792], ckv, col(R5 + 4), kvg[:, :], ALU.mult, ALU.mult).then_inc(S["ckvn_ready"], 1)
                    gathered(8)
                    v.wait_ge(S["g_ps"], 1)
                    v.tensor_tensor(mixT[:, 256:512], pj[1][:, 0:256], pr[:, 256:512], ALU.mult).then_inc(S["mix_ready"], 1)
                    y, yt = wk[:, 0:256], wk[:, 256:512]
                    for j in range(2):
                        js = slice(j * 128, (j + 1) * 128)
                        note(v.scalar_tensor_tensor(y[:, js], pr[:, js], col(DSK + j), pj[0][:, js], ALU.mult, ALU.add))
                    settled()
                    link(v.tensor_tensor(yt, y, y, ALU.mult))
                    link(v.tensor_scalar(yt, yt, GELU_A, 1.0, ALU.mult, ALU.add))
                    v.tensor_tensor(yt, yt, y, ALU.mult).then_inc(S["glu_in"], 1)
                    v.wait_ge(S["glu_th"], 1)
                    link(v.scalar_tensor_tensor(y, yt, 1.0, y, ALU.add, ALU.mult))
                    v.tensor_scalar(y, y, 0.5, None, ALU.mult).then_inc(S["yg_ready"], 1)
                    gathered(9)
                    v.wait_ge(S["z_th"], 2)
                    link(v.scalar_tensor_tensor(yt, wk[:, 512:768], 1.0, y, ALU.add, ALU.mult))
                    v.tensor_scalar(mixT[:, 0:256], yt, 0.5, None, ALU.mult).then_inc(S["mix_ready"], 1)
                    v.wait_ge(S["ckv_cached"], 2)
                    sc, am, nd, D_ = wk[:, 0:512], wk[:, 1024:1536], wk[:, 1536:2048], wk[:, 512:1024]
                    note(v.tensor_scalar(col(WSC, 4), pr[:, 1792:1796], 1.0 / 16, None, ALU.mult))
                    note(v.tensor_scalar(am, nd0[:, :], col(LIMP), NEG, ALU.is_ge, ALU.mult))
                    note(v.tensor_scalar(nd, nd0[:, :], col(B128), None, ALU.subtract))
                    settled()
                    link(v.scalar_tensor_tensor(nd, nd, -1.0, nd, ALU.mult, ALU.min))
                    v.wait_ge(S["relu_sb"], 1)
                    link(v.tensor_scalar(sc, wk[:, 2048:2560], col(WSC), None, ALU.mult))
                    for h in range(1, IH):
                        v.wait_ge(S["relu_sb"], h + 1)
                        link(v.scalar_tensor_tensor(sc, wk[:, 2048 + h * 512:2560 + h * 512], col(WSC + h), sc, ALU.mult, ALU.add))
                    link(v.tensor_tensor(sc, sc, am, ALU.add))
                    link(v.tensor_tensor(nd, am, nd, ALU.add))
                    gathered(10)
                    for r in range(TOPK // 8):
                        link(v.max(val[:, 0:8], sc))
                        link(v.match_replace(sc, val[:, 0:8], sc, GONE))
                        gathered(10 + (r + 1) * 6 // 16)
                    link(v.tensor_scalar(D_, sc, -2e38, NEG, ALU.is_gt, ALU.mult))
                    link(v.tensor_tensor(D_, D_, nd, ALU.add))

                    def scale_p(h):
                        v.wait_ge(S["exp_done"], h + 1)
                        link(v.reciprocal(col(RD + h), col(DEN + h)))
                        P = wk[:, 3072 + (h % 2) * 512:3584 + (h % 2) * 512]
                        v.tensor_scalar(P, P, col(RD + h), None, ALU.mult).then_inc(S["p_ready"], 1)
                    for h in range(AH):
                        v.wait_ge(S["lg_ps"], h + 1)
                        if h >= 2:
                            v.wait_ge(S["exp_done"], h - 1)
                        L = wk[:, 2048 + (h % 2) * 512:2560 + (h % 2) * 512]
                        v.scalar_tensor_tensor(L, D_, 2.0 ** (-8.0 * (h + 1) / AH), pw[:, (h % 2) * 512:(h % 2 + 1) * 512],
                                               ALU.mult, ALU.add).then_inc(S["lg_used"], 1)
                        v.wait_ge(S["lg_used"], h + 1)
                        v.tensor_reduce(col(NM + h), L, AXX, ALU.max, negate=True).then_inc(S["nmax"], 1)
                        if h >= 1:
                            scale_p(h - 1)
                        gathered(16 + h // 2)
                    scale_p(AH - 1)
                    gathered(20)
                    for n in range(2):
                        v.wait_ge(S["out_ps"], n + 1)
                        ns = slice(n * 512, (n + 1) * 512)
                        link(v.tensor_tensor(wk[:, ns], pj[n][:, :], mod(GATE1, n * 512, 512), ALU.mult))
                        v.tensor_tensor(xs[:, ns], xs[:, ns], wk[:, ns], ALU.add).then_inc(S["x1_ready"], 1)
                    v.wait_ge(S["x1_ready"], 2)
                    gathered(21)
                    v.wait_ge(S["ss2"], 1)
                    normed(SS2, RS2, SCALE2, SHIFT2, "h2_ready")
                    gathered(24)
                    v.wait_ge(S["s_ps"], 1)
                    s16 = pw[:, :].rearrange("p (f n) -> p f n", f=16)
                    r16 = wk[:, 2048:4096].rearrange("p (f n) -> p f n", f=16)
                    v16 = val[:, :].rearrange("p (f k) -> p f k", f=16)
                    i16 = vix[:, :].rearrange("p (f k) -> p f k", f=16)
                    for f in range(16):
                        note(v.max(v16[:, f, 0:8], s16[:, f, :]))
                    settled()
                    for f in range(16):
                        note(v.max_index(i16[:, f, 0:8], v16[:, f, 0:8], s16[:, f, :]))
                        note(v.match_replace(r16[:, f, :], v16[:, f, 0:8], s16[:, f, :], GONE))
                        if f % 8 == 7:
                            gathered(25 + f // 8)
                    settled()
                    for f in range(16):
                        note(v.max(v16[:, f, 8:16], r16[:, f, :]))
                    settled()
                    for f in range(16):
                        note(v.max_index(i16[:, f, 8:16], v16[:, f, 8:16], r16[:, f, :]))
                    settled()
                    gathered(27)
                    cand = wk[:, 0:2048].rearrange("p (h a b) -> p h a b", h=8, a=16)
                    va = val[:, 0:128].unsqueeze(2).broadcast_to([128, 128, 16]).rearrange("p (h a) b -> p h a b", h=8)
                    vb2 = val[:, 128:256].rearrange("p (h b) -> p h b", h=8).unsqueeze(2).broadcast_to([128, 8, 16, 16])
                    for h in range(PH):
                        note(v.tensor_tensor(cand[:, h], va[:, h], vb2[:, h], ALU.add))
                    settled()
                    c8 = wk[:, 0:2048].rearrange("p (h c) -> p h c", h=8)
                    d8 = wk[:, 2048:4096].rearrange("p (h c) -> p h c", h=8)
                    cv8 = cv[:, :].rearrange("p (h k) -> p h k", h=8)
                    cp8 = cpos[:, :].rearrange("p (h k) -> p h k", h=8)
                    for h in range(PH):
                        note(v.max(cv8[:, h, 0:8], c8[:, h, :]))
                    settled()
                    for h in range(PH):
                        note(v.max_index(cp8[:, h, 0:8], cv8[:, h, 0:8], c8[:, h, :]))
                        note(v.match_replace(d8[:, h, :], cv8[:, h, 0:8], c8[:, h, :], GONE))
                    settled()
                    gathered(28)
                    for h in range(PH):
                        note(v.max(cv8[:, h, 8:16], d8[:, h, :]))
                    settled()
                    for h in range(PH):
                        note(v.max_index(cp8[:, h, 8:16], cv8[:, h, 8:16], d8[:, h, :]))
                    settled()
                    gathered(29)
                    gw8 = gate_w[:, :].rearrange("p (h k) -> p h k", h=8)
                    v.tensor_tensor(gw8, cv8, cv8[:, :, 0:1].broadcast_to([128, 8, 16]), ALU.subtract).then_inc(S["top_ready"], 1)
                    pa, pb = hT[:, 768:896].bitcast(I32), hT[:, 896:1024].bitcast(I32)
                    af, bf, ixf = hT[:, 0:128], hT[:, 128:256], hT[:, 256:512]
                    e1, e2 = hT[:, 512:640], hT[:, 640:768]
                    cpi = cpos[:, :].bitcast(I32)
                    note(v.tensor_scalar(pa, cpi, 4, None, ALU.logical_shift_right))
                    note(v.tensor_scalar(pb, cpi, 15, None, ALU.bitwise_and))
                    note(v.tensor_copy(ixf, vix[:, :]))
                    settled()
                    note(v.tensor_copy(af, pa))
                    note(v.tensor_copy(bf, pb))
                    settled()
                    eq = wk[:, 0:2048].rearrange("p (e a) -> p e a", e=128)
                    eq4 = wk[:, 0:2048].rearrange("p (h j a) -> p h j a", h=8, j=16)
                    for src, half, dst in ((af, 0, e1), (bf, 1, e2)):
                        link(v.tensor_tensor(eq, src.unsqueeze(2).broadcast_to([128, 128, 16]),
                                             iota16[:, :].unsqueeze(1).broadcast_to([128, 128, 16]), ALU.is_equal))
                        keys = ixf[:, half * 128:(half + 1) * 128].rearrange("p (h a) -> p h a", h=8)
                        link(v.tensor_tensor(eq4, eq4, keys.unsqueeze(2).broadcast_to([128, 8, 16, 16]), ALU.mult))
                        link(v.tensor_reduce(dst, eq, AXX, ALU.add))
                        gathered(30)
                    link(v.tensor_scalar(e1, e1, float(NKEY), float(l * NEXP), ALU.mult, ALU.add))
                    link(v.tensor_tensor(e1, e1, e2, ALU.add))
                    link(v.tensor_copy(idx_w[:, :], e1))
                    v.wait_ge(S["gexp"], 1)
                    link(v.tensor_reduce(cols[:, V5:V5 + 8], gw8, AXX, ALU.add))
                    link(v.reciprocal(cols[:, V5:V5 + 8], cols[:, V5:V5 + 8]))
                    link(v.tensor_scalar(cols[:, V5:V5 + 8], cols[:, V5:V5 + 8], 0.5, None, ALU.mult))
                    v.tensor_tensor(gw8, gw8, cols[:, V5:V5 + 8].unsqueeze(2).broadcast_to([128, 8, 16]), ALU.mult).then_inc(S["routed"], 1)
                    v.wait_ge(S["routed"], 1)

                if mixers:
                    mixer()
                gathered(NBAT + 1)
                if g is not None:
                    v.wait_ge(S["mixed"], HK)
                    v.wait_ge(S["x1_loaded"], 16)
                    link(v.tensor_tensor(wk[:, 0:D], py[:, :], g2g[:, :], ALU.mult))
                    if g[0] < DEPTH - 1:
                        v.tensor_tensor(wk[:, D:2 * D], wk[:, 0:D], wk[:, 3 * D:4 * D], ALU.add).then_inc(S["xn_ready"], 1)
                    else:
                        link(v.tensor_tensor(wk[:, D:2 * D], wk[:, 0:D], wk[:, 3 * D:4 * D], ALU.add))
                        xn = wk[:, D:2 * D]
                        link(v.tensor_tensor_reduce(out=wk[:, 0:D], in0=xn, in1=xn, scale=1.0, scalar=0.0,
                                                    op0=ALU.mult, op1=ALU.add, accum_out=col(SS1)))
                        link(v.tensor_scalar(col(SS1), col(SS1), 1.0 / D, EPS, ALU.mult, ALU.add))
                        rsqrt(col(RS1), col(SS1), it[:, 2:3])
                        v.wait_ge(S["gain_in"], 16)
                        v.scalar_tensor_tensor(wk[:, D:2 * D], xn, col(RS1), wk[:, 2 * D:3 * D], ALU.mult,
                                               ALU.mult).then_inc(S["xn_ready"], 1)
                if mixers:
                    note(v.tensor_copy(h2g[:, :], hh[:, :]))
                    note(v.tensor_copy(g2g[:, :], mod(GATE2)))
                    note(v.tensor_copy(gate_g[:, :], gate_w[:, :]))
                    note(v.tensor_copy(idx_g[:, :], idx_w[:, :]))
                meet(v, "dve")
            legs(v, leg)

        @block.sync
        def _(sp):
            sp.wait_ge(consts, 16)

            def bcast(row, n=128):
                return row.partition_broadcast(n)

            def leg(l, b, mixers, g, before):
                wn = [0]
                users = [("mod_ps", i + 1) for i in range(12)] if is_first(b) else []
                users += [("proj_ps", i + 1) for i in range(4)] + [("out_ps", 1), ("out_ps", 2)]

                def weights(src, c0, width):
                    n = wn[0]
                    wn[0] += 1
                    if n >= 2:
                        sem, count = users[n - 2]
                        sp.wait_ge(S[sem], count)
                    sp.dma_start(wring[n % 2][:, 0:KT * width].rearrange("p (k c) -> p k c", k=KT),
                                 src.rearrange("(k p) c -> p k c", p=128)[:, :, c0:c0 + width]).then_inc(S[f"w_l{n % 2}"], 16)

                def par(dst, src):
                    sp.dma_start(dst, src, allow_slow_non_contiguous=True).then_inc(S["params"], 16)
                    npar[0] += 1
                npar = [0]
                if mixers:
                    if is_first(b):
                        sp.dma_start(sm[:, 312:320], A["c"].rearrange("o (k p) -> p (o k)", p=128),
                                     allow_slow_non_contiguous=True).then_inc(S["c_loaded"], 16)
                        for gg in range(2):
                            lo = 64 * gg
                            for j in range(2):
                                for i, name in ((0, "ssm_a_re_log"), (1, "ssm_a_im")):
                                    par(sm[lo:lo + 64, i * 8:(i + 1) * 8].rearrange("p (q j) -> p j q", q=4)[:, j],
                                        A[name][l].rearrange("(j q g) n -> j g n q", q=4, g=2)[j, gg])
                                par(sm[lo:lo + 64, 16:24].rearrange("p (q j) -> p j q", q=4)[:, j],
                                    A["ssm_log_dt"][l].rearrange("(j q g) -> j g q", q=4, g=2)[j, gg].partition_broadcast(64))
                            for at, name in ((0, "ssm_b_re"), (128, "ssm_b_im")):
                                for j in range(2):
                                    par(wk[lo:lo + 64, at:at + 128].rearrange("p (q j h) -> p j q h", q=4, j=2)[:, j],
                                        A[name][l].rearrange("(j q g) n h -> j g n q h", q=4, g=2)[j, gg])
                        for at, name in ((1024, "ssm_c_re"), (1152, "ssm_c_im")):
                            par(wk[:, at:at + 128].rearrange("p (j n) -> p j n", j=2),
                                A[name][l].rearrange("(j r) h n -> (r h) j n", j=2))
                        par(wk[:, 2048:2560].rearrange("p (h s) -> p h s", h=4), A["gmlp_w_sp"][l].rearrange("h t s -> t h s"))
                        par(wk[:, 1792:1856], A["peer_k1"][l])
                        par(wk[:, 1856:1920], A["peer_k2"][l])
                        par(wglu[:, :].rearrange("p (j n) -> p j n", j=2), A["ssm_w_glu"][l].rearrange("(j p) n -> p j n", p=128))
                        par(wuk[:, :].rearrange("p (a r) -> p a r", a=4), A["w_uk"][l].rearrange("(a b) d r -> (b d) a r", b=2))
                        par(wuv[:, :].rearrange("p (h d) -> p h d", h=8), A["w_uv"][l].rearrange("h r d -> r h d"))
                        par(cols[:, DSK:DSK + 2], A["ssm_d"][l].rearrange("(j p) -> p j", p=128))
                        par(cols[:, BGH:BGH + 2], A["ssm_b_glu"][l].rearrange("(j p) -> p j", p=128))
                        par(kvg[:, :], bcast(A["kv_norm_g"][l]))
                        par(bsp[0:1, :], A["gmlp_b_sp"][l].rearrange("(o h) t -> o (h t)", o=1))
                        par(modb[:, :], bcast(A["b_mod"][l]))
                        par(hh[:, :], bcast(A["norm1_g"][l]))
                        par(hT[:, :], bcast(A["norm2_g"][l]))
                        assert npar[0] == NPAR, npar
                    src = A["x"].rearrange("o s d -> (o s) d") if l == 0 else x_mid
                    sp.dma_start(xs[:, :], src[bass.ds(b * T, T), :]).then_inc(S["x_in"], 16)
                    if is_first(b):
                        for n in range(12):
                            weights(A["w_mod"][l], n * 512, 512)
                    for c0, width in GROUPS:
                        weights(A["w_in"][l], c0, width)
                    for name in ("w_out", "peer_w_q"):
                        for n in range(2):
                            weights(A[name][l], n * 512, 512)
                    sp.wait_ge(S["x1_ready"], 2)
                    sp.dma_start(x_mix[bass.ds(b * T, T), :], xs[:, :]).then_inc(S["x1_saved"], 16)
                if g is not None:
                    gl, gb = g
                    if mixers:
                        sp.wait_ge(S["routed"], 1)
                    sp.dma_start(wk[:, 3 * D:4 * D], x_mix[bass.ds(gb * T, T), :]).then_inc(S["x1_loaded"], 16)
                    if gl == DEPTH - 1:
                        sp.dma_start(wk[:, 2 * D:3 * D], bcast(A["final_g"])).then_inc(S["gain_in"], 16)
                    sp.wait_ge(S["xn_ready"], 1)
                    dst = (out.rearrange("o s d -> (o s) d") if gl == DEPTH - 1 else x_mid)[bass.ds(gb * T, T), :]
                    sp.dma_start(dst, wk[:, D:2 * D]).then_inc(S["x_stored"], 16)
                    sp.wait_ge(S["x_stored"], 16)
                if mixers:
                    sp.wait_ge(S["x1_saved"], 16)
                sp.wait_ge(arrive, 4)
                if debug and not (debug == "two" and is_first(b)):
                    dump = out.rearrange("o s d -> (o s) d")
                    for i, tile in enumerate((xs, hh, mixT)):
                        sp.dma_start(dump[i * 128:(i + 1) * 128, :], tile[:, :]).then_inc(S["debug"], 16)
                    sp.dma_start(dump[384:512, 0:128], gate_w[:, :]).then_inc(S["debug"], 16)
                    sp.dma_start(dump[384:512, 128:256], idx_w[:, :].bitcast(F32)).then_inc(S["debug"], 16)
                    sp.dma_start(dump[384:512, 256:512], val[:, :]).then_inc(S["debug"], 16)
                    sp.dma_start(dump[384:512, 512:1024], wk[:, 0:512]).then_inc(S["debug"], 16)
                    sp.wait_ge(S["debug"], 16 * 7)
                sp.sem_inc(arrive, -4)
                sp.sem_clear(range(nums[0], nums[-1] + 1))
                for s in go.values():
                    sp.sem_inc(s, 1)
            legs(sp, leg)


_INS = ["x", "c", "norm1_g", "norm2_g", "w_mod", "b_mod", "w_in", "ssm_a_re_log", "ssm_a_im", "ssm_b_re",
        "ssm_b_im", "ssm_c_re", "ssm_c_im", "ssm_d", "ssm_log_dt", "ssm_w_glu", "ssm_b_glu", "gmlp_w_sp",
        "gmlp_b_sp", "kv_norm_g", "w_uk", "w_uv", "w_out", "peer_w_q", "peer_k1", "peer_k2", "peer_u",
        "peer_v", "final_g"]


DEBUG = None


def kernel(**inputs):
    import numpy as np
    import concourse.bacc as bacc
    from concourse.bass_utils import run_bass_kernel_spmd

    nc = bacc.Bacc("TRN2", target_bir_lowering=False, num_devices=1)
    arrays, A = {}, {}
    for name in _INS:
        a = np.ascontiguousarray(inputs[name])
        arrays[f"in_{name}"] = a
        A[name] = nc.dram_tensor(f"in_{name}", a.shape, mybir.dt.from_np(a.dtype), kind="ExternalInput").ap()
    out = nc.dram_tensor("out", (1, SEQ, D), F32, kind="ExternalOutput").ap()
    build(nc, A, out, debug=DEBUG)
    r = run_bass_kernel_spmd(nc, [arrays], core_ids=[0])
    return r.results[0]["out"]
```

```python
import math
from contextlib import ExitStack

import concourse.bass as bass
from concourse import mybir

F32 = mybir.dt.float32
I32 = mybir.dt.int32
U32 = mybir.dt.uint32
ALU = mybir.AluOpType
ACT = mybir.ActivationFunctionType
AXX = mybir.AxisListType.X

D = 1024
T = 128
SEQ = 512
NB = SEQ // T
DEPTH = 2
KT = D // 128
EPS = 1e-6
IN_W = 1732
AH, AHD, RANK = 8, 64, 128
IH = 4
TOPK = 128
PH, PK, NKEY = 8, 16, 128
HK = PH * PK
NEXP = NKEY * NKEY
NR = 8
GB = 2
NBAT = HK // GB
AHEAD = NR // GB
LEAD = 2
ND = 4
MOD_EARLY = 9
NEG = -1e30
GONE = -3e38
GELU_A, GELU_S = 0.044715, math.sqrt(2.0 / math.pi)
C_V, C_Q, C_CKV, C_QI, C_KI, C_WI = 512, 768, 1280, 1408, 1664, 1728
GROUPS = [(0, 512), (512, 512), (1024, 512), (1536, IN_W - 1536)]
SHIFT1, SCALE1, GATE1, SHIFT2, SCALE2, GATE2 = range(6)

PACE = {
    "start": [4], "projected": [8, 10, 12, 14], "states": [16], "gated": [18],
    "picked": [20 + (r + 1) * 3 // 4 for r in range(16)],
    "heads": [32 + (h + 1) * 3 // 2 for h in range(8)],
    "values": [45], "x1": [47], "h2": [49], "queries": [51, 52],
    "routing": [54, 55, 57, 58, 60, 62],
}


PACE_FIRST = dict(
    PACE, mod=[3, 4, 5, 6, 7, 8, 9, 10, 10, 22, 25, 28], prepared=[3, 5, 6, 7, 8, 9, 9, 10, 10, 10], start=[10],
    projected=[10, 11, 13, 14])


def is_first(b):
    return isinstance(b, int) and b == 0


def upto(b, stage, i=0):
    return (PACE_FIRST if is_first(b) else PACE)[stage][i]


NAMES = """x_in ss1 h_ready hT_ps hT_sb proj_ps proj_sb ki_cached bu_ps bu_used prods y_ps glu_in glu_th
yg_ready z_ps z_th vn_ready ckvn_ready g_ps mix_ready ckvT_ps ckv_cached sc_ps relu_sb qa_ps qa_sb
lg_ps lg_used nmax exp_done p_ready pt_ps pt_sb o_ps o_sb yc_ps yc_sb out_ps x1_ready ss2 h2_ready
h2T_ps h2T_sb pq_ps pq_sb s_ps top_ready gexp routed chain act_pre act_th w_ready diag_ready dots
mixed xn_ready x_stored x1_loaded x1_saved cc_exp crep_ready e_ready e_ps mod_ps mod_sb gained b_loaded params scored gain2_in c_loaded w_l0 w_l1
gain_in state_re""".split()


def build(nc, A, out):
    ctx = ExitStack()
    with ctx:
        def sb(name, cols, dt=F32, rows=128):
            return ctx.enter_context(nc.sbuf_tensor(name, [rows, cols], dt))

        def ps(name, cols):
            return ctx.enter_context(nc.psum_tensor(name, [128, cols], F32))

        ringU = [sb(f"ringU{i}", D) for i in range(NR)]
        ringV = [sb(f"ringV{i}", D) for i in range(NR)]
        wring = [sb(f"wring{i}", KT * 512) for i in range(2)]
        modb = sb("modb", 6 * D)
        wk = sb("wk", 4 * D)
        xs, hh, hT = sb("xs", D), sb("hh", D), sb("hT", D)
        mixT = sb("mixT", D)
        pr = sb("pr", 3 * 512 + 260)
        h2g, g2g = sb("h2g", D), sb("g2g", D)
        cosT, sinT = sb("cosT", D), sb("sinT", D)
        BBre, BBim = sb("BBre", 256), sb("BBim", 256)
        CCre, nCre, nCim = sb("CCre", 256), sb("nCre", 256), sb("nCim", 256)
        wglu, wuk, wuv, wsT = sb("wglu", 512), sb("wuk", 512), sb("wuv", 512), sb("wsT", 512)
        kT, kvg, bsp = sb("kT", 128), sb("kvg", 128), sb("bsp", 512, rows=1)
        ckv_all, ckvT_all, kiT_all = sb("ckv_all", 512), sb("ckvT_all", 512), sb("kiT_all", 512)
        nd0 = sb("nd0", 512)
        ident = sb("ident", 128)
        diag = sb("diag", ND * 128)
        ones = sb("ones", 128, rows=1)
        gate_w, gate_g = sb("gate_w", HK), sb("gate_g", HK)
        idx_w, idx_g = sb("idx_w", HK, U32), sb("idx_g", HK, U32)
        val, vix = sb("val", 256), sb("vix", 256, U32)
        cv, cpos = sb("cv", HK), sb("cpos", HK, U32)
        m8 = sb("m8", 8)
        sm = pr[:, 0:40 * 8]
        iota16 = sb("iota16", 16)
        cols = sb("cols", 64)
        it = sb("it", 16, I32)
        state = sb("state", 16)
        abat, atmp = sb("abat", 2 * GB), sb("atmp", 2 * GB)
        wbat = sb("wbat", 2 * GB)
        py = ps("py", D)
        pj = [ps("pj0", 512), ps("pj1", 512)]
        pw = ps("pw", 4 * 512)
        x_mid = nc.dram_tensor("x_mid", [SEQ, D], F32, kind="Internal").ap()
        x_mix = nc.dram_tensor("x_mix", [SEQ, D], F32, kind="Internal").ap()
        ux = A["peer_u"].rearrange("l e d -> (l e) d")
        vx = A["peer_v"].rearrange("l e d -> (l e) d")

        def col(i, n=1):
            return cols[:, i:i + n]
        SS1, RS1, SS2, RS2, B128, LIMP, PCOL, HALF, ODD = range(9)
        V5, R5, MU, DEN, NM, RD, WSC, DSK, BGH, CACT, EVEN = 9, 14, 19, 23, 31, 39, 47, 51, 53, 55, 63

        S = {n: ctx.enter_context(nc.semaphore(n)) for n in NAMES}
        nums = sorted(s.num for s in S.values())
        assert nums == list(range(nums[0], nums[0] + len(nums)))
        arrive = ctx.enter_context(nc.semaphore("arrive"))
        go = {e: ctx.enter_context(nc.semaphore("go_" + e)) for e in ("pool", "act", "pe", "dve")}
        landU = [ctx.enter_context(nc.semaphore(f"landU{i}")) for i in range(NR)]
        landV = [ctx.enter_context(nc.semaphore(f"landV{i}")) for i in range(NR)]
        consts = ctx.enter_context(nc.semaphore("consts"))
        LAND = 16 * HK // NR
        NPAR = 33

        def meet(eng, name):
            eng.drain().then_inc(arrive, 1)
            eng.wait_ge(go[name], 1)
            eng.sem_inc(go[name], -1)

        def legs(eng, leg):
            leg(0, 0, True, None, 0)
            with eng.Fori(1, NB) as b:
                leg(0, b, True, (0, b - 1), (b - 1) * LAND)
            leg(1, 0, True, (0, NB - 1), (NB - 1) * LAND)
            with eng.Fori(1, NB) as b:
                leg(1, b, True, (1, b - 1), (b + (NB - 1)) * LAND)
            leg(1, 0, False, (1, NB - 1), (2 * NB - 1) * LAND)

        def parameter_loads(eng, l):
            npar = [0]

            def par(dst, src):
                eng.dma_start(dst, src, allow_slow_non_contiguous=True).then_inc(S["params"], 16)
                npar[0] += 1
            for gg in range(2):
                lo = 64 * gg
                for j in range(2):
                    for i, name in ((0, "ssm_a_re_log"), (1, "ssm_a_im")):
                        par(sm[lo:lo + 64, i * 8:(i + 1) * 8].rearrange("p (q j) -> p j q", q=4)[:, j],
                            A[name][l].rearrange("(j q g) n -> j g n q", q=4, g=2)[j, gg])
                    par(sm[lo:lo + 64, 16:24].rearrange("p (q j) -> p j q", q=4)[:, j],
                        A["ssm_log_dt"][l].rearrange("(j q g) -> j g q", q=4, g=2)[j, gg].partition_broadcast(64))
                for at, name in ((0, "ssm_b_re"), (128, "ssm_b_im")):
                    for j in range(2):
                        par(wk[lo:lo + 64, at:at + 128].rearrange("p (q j h) -> p j q h", q=4, j=2)[:, j],
                            A[name][l].rearrange("(j q g) n h -> j g n q h", q=4, g=2)[j, gg])
            for at, name in ((1024, "ssm_c_re"), (1152, "ssm_c_im")):
                par(wk[:, at:at + 128].rearrange("p (j n) -> p j n", j=2),
                    A[name][l].rearrange("(j r) h n -> (r h) j n", j=2))
            par(wk[:, 2048:2560].rearrange("p (h s) -> p h s", h=4), A["gmlp_w_sp"][l].rearrange("h t s -> t h s"))
            par(wk[:, 1792:1856], A["peer_k1"][l])
            par(wk[:, 1856:1920], A["peer_k2"][l])
            par(wglu[:, :].rearrange("p (j n) -> p j n", j=2), A["ssm_w_glu"][l].rearrange("(j p) n -> p j n", p=128))
            par(wuk[:, :].rearrange("p (a r) -> p a r", a=4), A["w_uk"][l].rearrange("(a b) d r -> (b d) a r", b=2))
            par(wuv[:, :].rearrange("p (h d) -> p h d", h=8), A["w_uv"][l].rearrange("h r d -> r h d"))
            par(cols[:, DSK:DSK + 2], A["ssm_d"][l].rearrange("(j p) -> p j", p=128))
            par(cols[:, BGH:BGH + 2], A["ssm_b_glu"][l].rearrange("(j p) -> p j", p=128))
            par(kvg[:, :], A["kv_norm_g"][l].partition_broadcast(128))
            par(bsp[0:1, :], A["gmlp_b_sp"][l].rearrange("(o h) t -> o (h t)", o=1))
            par(hh[:, :], A["norm1_g"][l].partition_broadcast(128))
            assert npar[0] == NPAR, npar

        block = ctx.enter_context(nc.Block())

        @block.gpsimd
        def _(pool):
            pool.memset(ident[:, :], 0.0).then_inc(consts, 1)
            pool.memset(ones[:, :], 1.0).then_inc(consts, 1)
            pool.memset(ckv_all[:, :], 0.0).then_inc(consts, 1)
            pool.memset(ckvT_all[:, :], 0.0).then_inc(consts, 1)
            pool.memset(kiT_all[:, :], 0.0).then_inc(consts, 1)
            pool.iota(wk[:, 0:512].bitcast(I32), pattern=[[1, 512]], base=0, channel_multiplier=-1).then_inc(consts, 1)
            pool.iota(it[:, 0:1], pattern=[[0, 1]], base=0, channel_multiplier=1).then_inc(consts, 1)
            pool.iota(wk[:, 512:528].bitcast(I32), pattern=[[1, 16]], base=0, channel_multiplier=0).then_inc(consts, 1)
            pool.wait_ge(consts, 8)
            pool.affine_select(out=ident[:, :], in_=ident[:, :], compare_op=ALU.not_equal, fill=1.0,
                               base=0, pattern=[[-1, 128]], channel_multiplier=1).then_inc(consts, 1)

            def leg(l, b, mixers, g, before):
                def rows(ring, land, src, j, freed, idx):
                    for k in range(j * GB, (j + 1) * GB):
                        if k >= NR and g is not None:
                            pool.wait_ge(freed, k - NR + 1)
                        pool.indirect_dma_start(
                            out=ring[k % NR][:, :], out_offset=None, in_=src,
                            in_offset=bass.IndirectOffsetOnAxis(ap=idx[:, k % HK:k % HK + 1], axis=0),
                        ).then_inc(land[k % NR], 16)
                if g is not None:
                    for j in range(AHEAD, AHEAD + LEAD):
                        rows(ringU, landU, ux, j, S["dots"], idx_g)
                    for j in range(AHEAD, NBAT):
                        if j + LEAD < NBAT:
                            rows(ringU, landU, ux, j + LEAD, S["dots"], idx_g)
                        rows(ringV, landV, vx, j, S["mixed"], idx_g)
                if mixers:
                    pool.wait_ge(S["routed"], 1)
                    for j in range(NBAT, NBAT + AHEAD):
                        rows(ringU, landU, ux, j, S["dots"], idx_w)
                    for j in range(NBAT, NBAT + AHEAD):
                        rows(ringV, landV, vx, j, S["mixed"], idx_w)
                meet(pool, "pool")
            legs(pool, leg)

        @block.scalar
        def _(a):
            a.wait_ge(consts, 16)

            def leg(l, b, mixers, g, before):
                done = [0]

                def gathered(n):
                    if g is None:
                        return
                    while done[0] < n:
                        j = done[0]
                        if j < NBAT:
                            a.wait_ge(S["act_pre"], j + 1)
                            a.activation(atmp[:, (j % 2) * GB:(j % 2 + 1) * GB], atmp[:, (j % 2) * GB:(j % 2 + 1) * GB],
                                         ACT.Tanh, scale=GELU_S).then_inc(S["act_th"], 1)
                        if j >= 1:
                            a.wait_ge(S["w_ready"], j)
                            for k in range((j - 1) * GB, j * GB):
                                if k >= ND:
                                    a.wait_ge(S["mixed"], k - ND + 1)
                                a.activation(diag[:, (k % ND) * 128:(k % ND + 1) * 128], ident[:, :], ACT.Copy,
                                             scale=wbat[:, k % (2 * GB):k % (2 * GB) + 1]).then_inc(S["diag_ready"], 1)
                        done[0] += 1

                def copy(dst, src, sem):
                    a.activation(dst, src, ACT.Copy).then_inc(S[sem], 1)

                def modulation(n0, n1):
                    for n in range(n0, n1):
                        a.wait_ge(S["mod_ps"], n + 1)
                        copy(modb[:, n * 512:(n + 1) * 512], pj[n % 2][:, :], "mod_sb")
                        gathered(upto(b, "mod", n))

                if mixers:
                    if is_first(b):
                        a.wait_ge(S["c_loaded"], 16)
                        a.activation(cols[:, EVEN - 8:EVEN], sm[:, 312:320], ACT.Exp, scale=-1.0).then_inc(S["cc_exp"], 1)
                    if is_first(b):
                        parameter_loads(a, l)
                        modulation(0, MOD_EARLY)
                        a.wait_ge(S["gained"], 1)
                    a.wait_ge(S["x_in"], 16)
                    a.activation(hh[:, :], xs[:, :], ACT.Square, accum_out=col(SS1)).then_inc(S["ss1"], 1)
                    gathered(upto(b, "start"))
                    for n in range(2):
                        a.wait_ge(S["hT_ps"], n + 1)
                        copy(hT[:, n * 512:(n + 1) * 512], pj[n][:, :], "hT_sb")
                    for n in range(4):
                        a.wait_ge(S["proj_ps"], n + 1)
                        wide = 512 if n < 3 else 260
                        copy(pr[:, n * 512:n * 512 + wide], pj[n % 2][:, 0:wide], "proj_sb")
                        if n < 3:
                            gathered(upto(b, "projected", n))
                    copy(kiT_all[:, bass.ds(b * T, T)], pj[1][:, 128:256], "ki_cached")
                    gathered(upto(b, "states"))
                    a.wait_ge(S["ckvT_ps"], 1)
                    copy(ckvT_all[:, bass.ds(b * T, T)], pj[1][:, 256:384], "ckv_cached")
                    copy(ckv_all[:, bass.ds(b * T, T)], wk[:, 1664:1792], "ckv_cached")
                    a.wait_ge(S["glu_in"], 1)
                    a.activation(wk[:, 256:512], wk[:, 256:512], ACT.Tanh, scale=GELU_S).then_inc(S["glu_th"], 1)
                    gathered(upto(b, "gated"))
                    a.wait_ge(S["z_ps"], 1)
                    for j in range(2):
                        a.activation(wk[:, 512 + j * 128:640 + j * 128], pj[0][:, 256 + j * 128:384 + j * 128], ACT.Tanh,
                                     scale=0.5, bias=col(BGH + j)).then_inc(S["z_th"], 1)
                    for h in range(IH):
                        a.wait_ge(S["sc_ps"], h + 1)
                        a.activation(wk[:, 2048 + h * 512:2560 + h * 512], pw[:, h * 512:(h + 1) * 512],
                                     ACT.Relu).then_inc(S["relu_sb"], 1)
                    for n in range(2):
                        a.wait_ge(S["qa_ps"], n + 1)
                        a.activation(hh[:, n * 512:(n + 1) * 512], pj[n][:, :], ACT.Copy,
                                     scale=AHD ** -0.5).then_inc(S["qa_sb"], 1)
                    if is_first(b):
                        modulation(MOD_EARLY, 12)
                    gathered(upto(b, "picked", 15))

                    def evac_p(h):
                        a.wait_ge(S["pt_ps"], h + 1)
                        if h >= 2:
                            a.wait_ge(S["o_ps"], h - 1)
                        copy(hT[:, (h % 2) * 512:(h % 2 + 1) * 512], pj[h % 2][:, :], "pt_sb")
                        if h in (3, 7):
                            a.wait_ge(S["o_ps"], h + 1)
                            if h == 3:
                                a.wait_ge(S["mix_ready"], 2)
                            copy(pr[:, (h // 4) * 512:(h // 4 + 1) * 512], pw[:, 1024:1536], "o_sb")
                    for h in range(AH):
                        a.wait_ge(S["nmax"], h + 1)
                        if h >= 2:
                            a.wait_ge(S["pt_ps"], h - 1)
                        a.activation(wk[:, 3072 + (h % 2) * 512:3584 + (h % 2) * 512], wk[:, 2048 + (h % 2) * 512:2560 + (h % 2) * 512],
                                     ACT.Exp, bias=col(NM + h), accum_out=col(DEN + h)).then_inc(S["exp_done"], 1)
                        if h >= 1:
                            evac_p(h - 1)
                        gathered(upto(b, "heads", h))
                    evac_p(AH - 1)
                    a.wait_ge(S["yc_ps"], 1)
                    copy(mixT[:, 512:1024], pw[:, 1536:2048], "yc_sb")
                    gathered(upto(b, "values"))
                    a.wait_ge(S["x1_ready"], 2)
                    gathered(upto(b, "x1"))
                    a.activation(wk[:, 1024:2048], xs[:, :], ACT.Square, accum_out=col(SS2)).then_inc(S["ss2"], 1)
                    gathered(upto(b, "h2"))
                    for n in range(2):
                        a.wait_ge(S["h2T_ps"], n + 1)
                        copy(hT[:, n * 512:(n + 1) * 512], pj[n][:, :], "h2T_sb")
                    gathered(upto(b, "queries", 0))
                    for n in range(2):
                        a.wait_ge(S["pq_ps"], n + 1)
                        copy(pr[:, n * 512:(n + 1) * 512], pj[n][:, :], "pq_sb")
                        if n == 0:
                            gathered(upto(b, "queries", 1))
                    gathered(upto(b, "routing", 4))
                    a.wait_ge(S["top_ready"], 1)
                    a.activation(gate_w[:, :], gate_w[:, :], ACT.Exp).then_inc(S["gexp"], 1)
                gathered(NBAT + 1)
                meet(a, "act")
            legs(a, leg)

        @block.tensor
        def _(t):
            t.wait_ge(consts, 9)

            def leg(l, b, mixers, g, before):
                done = [0]

                def gathered(n):
                    if g is None:
                        return
                    while done[0] < n:
                        j = done[0]
                        if j >= 1:
                            for k in range((j - 1) * GB, j * GB):
                                t.wait_ge(S["diag_ready"], k + 1)
                                t.wait_ge(landV[k % NR], before + 16 * (k // NR + 1))
                                for c in range(2):
                                    mm = t.matmul(py[:, c * 512:(c + 1) * 512], diag[:, (k % ND) * 128:(k % ND + 1) * 128],
                                                  ringV[k % NR][:, c * 512:(c + 1) * 512], start=k == 0, stop=k == HK - 1)
                                mm.then_inc(S["mixed"], 1)
                        done[0] += 1

                def turn(dst, src, last=None):
                    m = t.transpose(dst, src, ident[:, :])
                    if last:
                        m.then_inc(S[last], 1)

                wn = [0]

                def weights():
                    n = wn[0]
                    wn[0] += 1
                    if is_first(b):
                        t.wait_ge(S[f"w_l{n % 2}"], 16 * (n // 2 + 1))
                    elif n >= 2:
                        t.wait_ge(S[f"w_l{n % 2}"], 16 * (n // 2))
                    return wring[n % 2]

                def modulation(n0, n1, crep):
                    for n in range(n0, n1):
                        wt = weights()
                        if n >= 2:
                            t.wait_ge(S["mod_sb"], n - 1)
                        for k in range(KT):
                            t.matmul(pj[n % 2][:, :], crep[:, k * 128:(k + 1) * 128], wt[:, k * 512:(k + 1) * 512],
                                     start=k == 0, stop=False)
                        t.matmul(pj[n % 2][:, :], ones[0:1, :], modb[0:1, n * 512:(n + 1) * 512],
                                 start=False, stop=True).then_inc(S["mod_ps"], 1)
                        gathered(upto(b, "mod", n) - 1)

                if mixers:
                    if is_first(b):
                        t.wait_ge(S["crep_ready"], 1)
                        t.wait_ge(S["b_loaded"], 16)
                        modulation(0, MOD_EARLY - 1, mixT)
                        t.wait_ge(S["e_ready"], 1)
                        for i in range(2):
                            turn(pw[:, i * 128:(i + 1) * 128], wk[:, 512 + i * 128:640 + i * 128])
                            turn(pw[:, 256 + i * 128:384 + i * 128], wk[:, 768 + i * 128:896 + i * 128])
                            turn(pw[:, 512 + i * 128:640 + i * 128], wk[:, 1280 + i * 128:1408 + i * 128])
                            turn(pw[:, 768 + i * 128:896 + i * 128], wk[:, 1536 + i * 128:1664 + i * 128])
                        for h in range(4):
                            turn(pw[:, 1024 + h * 128:1152 + h * 128], wk[:, 2048 + h * 128:2176 + h * 128])
                        turn(pw[:, 1536:1664], wk[:, 1792:1920], "e_ps")
                        modulation(MOD_EARLY - 1, MOD_EARLY, mixT)
                        t.wait_ge(S["mod_sb"], MOD_EARLY)
                    gathered(3)
                    t.wait_ge(S["h_ready"], 1)
                    for k in range(KT):
                        turn(pj[k // 4][:, (k % 4) * 128:(k % 4 + 1) * 128], hh[:, k * 128:(k + 1) * 128],
                             "hT_ps" if k % 4 == 3 else None)
                    t.wait_ge(S["hT_sb"], 2)

                    def across(dst, wt, gc, c0, width, last=None):
                        for k in range(KT):
                            mm = t.matmul(dst, wt[:, k * gc + c0:k * gc + c0 + width], hT[:, k * 128:(k + 1) * 128],
                                          start=k == 0, stop=k == KT - 1)
                        return mm

                    def along(dst, wt, gc, c0, width):
                        for k in range(KT):
                            mm = t.matmul(dst, hT[:, k * 128:(k + 1) * 128], wt[:, k * gc + c0:k * gc + c0 + width],
                                          start=k == 0, stop=k == KT - 1)
                        return mm

                    wt = weights()
                    for f in range(4):
                        mm = across(pj[0][:, f * 128:(f + 1) * 128], wt, 512, f * 128, 128)
                    mm.then_inc(S["proj_ps"], 1)
                    gathered(upto(b, "projected", 0) - 1)
                    wt = weights()
                    along(pj[1][:, 0:256], wt, 512, 0, 256)
                    for f in range(2):
                        mm = across(pj[1][:, 256 + f * 128:384 + f * 128], wt, 512, 256 + f * 128, 128)
                    mm.then_inc(S["proj_ps"], 1)
                    t.wait_ge(S["proj_sb"], 1)
                    for ri, BB in enumerate((BBre, BBim)):
                        for j in range(2):
                            for q in range(4):
                                mm = t.matmul(pw[:, q * 512 + ri * 256 + j * 128:q * 512 + ri * 256 + (j + 1) * 128],
                                              BB[32 * q:32 * q + 32, j * 128:(j + 1) * 128],
                                              pr[32 * q:32 * q + 32, j * 128:(j + 1) * 128], start=True, stop=True)
                    mm.then_inc(S["bu_ps"], 1)
                    gathered(upto(b, "projected", 1) - 1)
                    wt = weights()
                    for f in range(2):
                        across(pj[0][:, f * 128:(f + 1) * 128], wt, 512, f * 128, 128)
                    along(pj[0][:, 256:384], wt, 512, 256, 128)
                    across(pj[0][:, 384:512], wt, 512, 384, 128).then_inc(S["proj_ps"], 1)
                    gathered(upto(b, "projected", 2) - 1)
                    wt = weights()
                    gc = GROUPS[3][1]
                    t.wait_ge(S["proj_sb"], 2)
                    across(pj[1][:, 0:128], wt, gc, 0, 128)
                    across(pj[1][0:64, 128:256], wt, gc, 128, 64)
                    across(pj[1][64:128, 128:256], wt, gc, 128, 64)
                    along(pj[1][:, 256:260], wt, gc, 192, 4).then_inc(S["proj_ps"], 1)
                    gathered(upto(b, "projected", 3) - 1)
                    t.wait_ge(S["prods"], 1)
                    t.wait_ge(S["proj_sb"], 3)
                    for j in range(2):
                        for q in range(4):
                            m = q * 2 + j
                            dst = pj[0][32 * q:32 * q + 32, j * 128:(j + 1) * 128]
                            cs = slice(j * 128 + 32 * q, j * 128 + 32 * q + 32)
                            for i, (C, at) in enumerate(((CCre, 0), (nCre, 2048), (nCim, 1024), (nCim, 3072))):
                                mm = t.matmul(dst, C[:, cs], wk[:, at + m * 128:at + (m + 1) * 128], start=i == 0, stop=i == 3)
                    mm.then_inc(S["y_ps"], 1)
                    gathered(upto(b, "states") - 1)
                    t.wait_ge(S["vn_ready"], 1)
                    t.wait_ge(S["ki_cached"], 1)
                    for h in range(4):
                        dst = pj[1][64 * (h % 2):64 * (h % 2) + 64, (h // 2) * 128:(h // 2 + 1) * 128]
                        t.matmul(dst, wk[:, 1024 + h * 64:1088 + h * 64], wsT[:, h * 128:(h + 1) * 128], start=True, stop=False)
                        mm = t.matmul(dst, ones[0:1, 0:64], bsp[0:1, h * 128:(h + 1) * 128], start=False, stop=True)
                    mm.then_inc(S["g_ps"], 1)
                    t.wait_ge(S["ckvn_ready"], 1)
                    t.wait_ge(S["mix_ready"], 1)
                    turn(pj[1][:, 256:384], wk[:, 1664:1792], "ckvT_ps")
                    gathered(upto(b, "gated") - 1)
                    t.wait_ge(S["yg_ready"], 1)
                    for jo in range(2):
                        for ji in range(2):
                            mm = t.matmul(pj[0][:, 256 + jo * 128:384 + jo * 128],
                                          wglu[:, ji * 256 + jo * 128:ji * 256 + (jo + 1) * 128],
                                          wk[:, ji * 128:(ji + 1) * 128], start=ji == 0, stop=ji == 1)
                    mm.then_inc(S["z_ps"], 1)
                    t.wait_ge(S["bu_used"], 1)
                    for h in range(IH):
                        lo = 64 * (h % 2)
                        at = 1408 if h < 2 else 1536
                        t.matmul(pw[:, h * 512:(h + 1) * 512], pr[lo:lo + 64, at:at + 128], kiT_all[lo:lo + 64, :],
                                 start=True, stop=True).then_inc(S["sc_ps"], 1)
                    t.wait_ge(S["z_th"], 2)
                    t.wait_ge(S["ckv_cached"], 2)
                    for n in range(2):
                        for i in range(4):
                            at = 768 + i * 128 if i < 2 else 1024 + (i - 2) * 128
                            mm = t.matmul(pj[n][:, i * 128:(i + 1) * 128], wuk[64 * n:64 * n + 64, i * 128:(i + 1) * 128],
                                          pr[64 * n:64 * n + 64, at:at + 128], start=True, stop=True)
                        mm.then_inc(S["qa_ps"], 1)
                    if is_first(b):
                        t.wait_ge(S["qa_sb"], 2)
                        t.wait_ge(S["crep_ready"], 2)
                        modulation(MOD_EARLY, 12, hT)
                        t.wait_ge(S["mod_sb"], 12)
                    gathered(upto(b, "picked", 15) - 1)
                    t.wait_ge(S["relu_sb"], 4)
                    t.wait_ge(S["qa_sb"], 2)

                    def logits(h):
                        if h >= 2:
                            t.wait_ge(S["lg_used"], h - 1)
                        q = hh[:, (h % 2) * 512 + (h // 2) * 128:(h % 2) * 512 + (h // 2 + 1) * 128]
                        t.matmul(pw[:, (h % 2) * 512:(h % 2 + 1) * 512], q, ckvT_all[:, :],
                                 start=True, stop=True).then_inc(S["lg_ps"], 1)

                    def values(h):
                        t.wait_ge(S["p_ready"], h + 1)
                        if h >= 2:
                            t.wait_ge(S["pt_sb"], h - 1)
                        for s in range(4):
                            turn(pj[h % 2][:, s * 128:(s + 1) * 128], wk[:, 3072 + (h % 2) * 512 + s * 128:3200 + (h % 2) * 512 + s * 128],
                                 "pt_ps" if s == 3 else None)
                        t.wait_ge(S["pt_sb"], h + 1)
                        if h == 4:
                            t.wait_ge(S["o_sb"], 1)
                        for s in range(4):
                            mm = t.matmul(pw[:, 1024 + (h % 4) * 128:1152 + (h % 4) * 128], ckv_all[:, s * 128:(s + 1) * 128],
                                          hT[:, (h % 2) * 512 + s * 128:(h % 2) * 512 + (s + 1) * 128], start=s == 0, stop=s == 3)
                        mm.then_inc(S["o_ps"], 1)
                    for h in range(AH):
                        logits(h)
                        if h >= 1:
                            values(h - 1)
                        gathered(upto(b, "heads", h) - 1)
                    values(AH - 1)
                    t.wait_ge(S["o_sb"], 2)
                    for h in range(AH):
                        mm = t.matmul(pw[64 * (h % 2):64 * (h % 2) + 64, 1536 + (h // 2) * 128:1664 + (h // 2) * 128],
                                      wuv[:, h * 64:(h + 1) * 64], pr[:, h * 128:(h + 1) * 128], start=True, stop=True)
                    mm.then_inc(S["yc_ps"], 1)
                    gathered(upto(b, "values") - 1)
                    t.wait_ge(S["yc_sb"], 1)
                    for n in range(2):
                        wt = weights()
                        for k in range(KT):
                            mm = t.matmul(pj[n][:, :], mixT[:, k * 128:(k + 1) * 128], wt[:, k * 512:(k + 1) * 512],
                                          start=k == 0, stop=k == KT - 1)
                        mm.then_inc(S["out_ps"], 1)
                    gathered(upto(b, "x1") - 1)
                    t.wait_ge(S["h2_ready"], 1)
                    for k in range(KT):
                        turn(pj[k // 4][:, (k % 4) * 128:(k % 4 + 1) * 128], hh[:, k * 128:(k + 1) * 128],
                             "h2T_ps" if k % 4 == 3 else None)
                    gathered(upto(b, "h2") - 1)
                    t.wait_ge(S["h2T_sb"], 2)
                    for n in range(2):
                        wt = weights()
                        for f in range(4):
                            mm = across(pj[n][:, f * 128:(f + 1) * 128], wt, 512, f * 128, 128)
                        mm.then_inc(S["pq_ps"], 1)
                        gathered(upto(b, "queries", n) - 1)
                    t.wait_ge(S["pq_sb"], 2)
                    for half in range(2):
                        for f in range(PH):
                            mm = t.matmul(pw[:, (half * 8 + f) * 128:(half * 8 + f + 1) * 128], pr[64 * half:64 * half + 64, f * 128:(f + 1) * 128],
                                          kT[64 * half:64 * half + 64, :], start=True, stop=True)
                    mm.then_inc(S["s_ps"], 1)
                    gathered(upto(b, "routing", 4) - 1)
                gathered(NBAT + 1)
                meet(t, "pe")
            legs(t, leg)

        @block.vector
        def _(v):
            v.wait_ge(consts, 9)
            v.tensor_copy(nd0[:, :], wk[:, 0:512].bitcast(I32)).then_inc(consts, 1)
            v.tensor_copy(col(PCOL), it[:, 0:1]).then_inc(consts, 1)
            v.tensor_copy(iota16[:, :], wk[:, 512:528].bitcast(I32)).then_inc(consts, 1)
            v.tensor_scalar(it[:, 1:2], it[:, 0:1], 4, 1, ALU.logical_shift_right, ALU.bitwise_and).then_inc(consts, 1)
            v.wait_ge(consts, 13)
            v.tensor_scalar(col(HALF), col(PCOL), 64.0, None, ALU.is_ge).then_inc(consts, 1)
            v.tensor_copy(col(ODD), it[:, 1:2]).then_inc(consts, 1)
            v.wait_ge(consts, 15)
            v.tensor_scalar(col(EVEN), col(ODD), -1.0, 1.0, ALU.mult, ALU.add).then_inc(consts, 1)
            v.wait_ge(consts, 16)

            def leg(l, b, mixers, g, before):
                done, chained = [0], [0]

                def link(ins):
                    chained[0] += 1
                    ins.then_inc(S["chain"], 1)
                    v.wait_ge(S["chain"], chained[0])

                def note(ins):
                    chained[0] += 1
                    ins.then_inc(S["chain"], 1)

                def settled():
                    v.wait_ge(S["chain"], chained[0])

                def weigh(j):
                    v.wait_ge(S["act_th"], j + 1)
                    s = slice((j % 2) * GB, (j % 2 + 1) * GB)
                    link(v.scalar_tensor_tensor(wbat[:, s], atmp[:, s], 1.0, abat[:, s], ALU.add, ALU.mult))
                    v.tensor_tensor(wbat[:, s], wbat[:, s], gate_g[:, j * GB:(j + 1) * GB], ALU.mult).then_inc(S["w_ready"], 1)

                def gathered(n):
                    if g is None:
                        return
                    while done[0] < n:
                        j = done[0]
                        if j < NBAT:
                            s = slice((j % 2) * GB, (j % 2 + 1) * GB)
                            for k in range(j * GB, (j + 1) * GB):
                                v.wait_ge(landU[k % NR], before + 16 * (k // NR + 1))
                                c = k % (2 * GB)
                                v.tensor_tensor_reduce(out=ringU[k % NR][:, :], in0=ringU[k % NR][:, :], in1=h2g[:, :],
                                                       scale=1.0, scalar=0.0, op0=ALU.mult, op1=ALU.add,
                                                       accum_out=abat[:, c:c + 1]).then_inc(S["dots"], 1)
                            v.wait_ge(S["dots"], (j + 1) * GB)
                            link(v.tensor_tensor(atmp[:, s], abat[:, s], abat[:, s], ALU.mult))
                            link(v.tensor_scalar(atmp[:, s], atmp[:, s], GELU_A, 1.0, ALU.mult, ALU.add))
                            v.tensor_tensor(atmp[:, s], atmp[:, s], abat[:, s], ALU.mult).then_inc(S["act_pre"], 1)
                        if j >= 1:
                            if j >= 3:
                                v.wait_ge(S["diag_ready"], (j - 2) * GB)
                            weigh(j - 1)
                        done[0] += 1

                def rsqrt(dst, src, bits):
                    tmp = bits.bitcast(F32)
                    link(v.tensor_scalar(bits, src.bitcast(I32), 1, None, ALU.logical_shift_right))
                    link(v.tensor_scalar(dst.bitcast(I32), bits, -1.0, float(0x5f3759df), ALU.mult, ALU.add))
                    for _ in range(3):
                        link(v.tensor_tensor(tmp, dst, dst, ALU.mult))
                        link(v.tensor_tensor(tmp, tmp, src, ALU.mult))
                        link(v.tensor_scalar(tmp, tmp, -0.5, 1.5, ALU.mult, ALU.add))
                        link(v.tensor_tensor(dst, dst, tmp, ALU.mult))

                def sm8(i):
                    return sm[:, i * 8:(i + 1) * 8]

                def exp8(dst, x, lo, hi):
                    n, r, p, q = sm8(24), sm8(25), sm8(26), sm8(27)
                    link(v.tensor_scalar(r, x, lo, hi, ALU.max, ALU.min))
                    link(v.tensor_scalar(n, r, 1.4426950408889634, None, ALU.mult))
                    link(v.tensor_scalar(n, n, 12582912.0, None, ALU.add))
                    link(v.tensor_scalar(n, n, 12582912.0, None, ALU.subtract))
                    link(v.scalar_tensor_tensor(r, n, -0.693359375, r, ALU.mult, ALU.add))
                    link(v.scalar_tensor_tensor(r, n, 2.12194440e-4, r, ALU.mult, ALU.add))
                    link(v.tensor_scalar(p, r, 1.0 / 5040, 1.0 / 720, ALU.mult, ALU.add))
                    for c in (1.0 / 120, 1.0 / 24, 1.0 / 6, 0.5, 1.0, 1.0):
                        link(v.tensor_tensor(p, p, r, ALU.mult))
                        link(v.tensor_scalar(p, p, c, None, ALU.add))
                    link(v.tensor_scalar(n, n, 127.0, None, ALU.add))
                    link(v.tensor_copy(q.bitcast(I32), n))
                    link(v.tensor_scalar(q.bitcast(I32), q.bitcast(I32), 23, None, ALU.logical_shift_left))
                    link(v.tensor_tensor(dst, p, q, ALU.mult))

                def parameters():
                    v.wait_ge(S["cc_exp"], 1)
                    e = cols[:, EVEN - 8:EVEN]
                    link(v.tensor_scalar(e, e, 1.0, None, ALU.add))
                    link(v.reciprocal(e, e))
                    link(v.tensor_tensor(e, e, sm[:, 312:320], ALU.mult))
                    v.tensor_copy(mixT[:, :].rearrange("p (k m) -> p k m", k=KT),
                                  spread_c()).then_inc(S["crep_ready"], 1)
                    gathered(upto(b, "prepared", 0))
                    gathered(upto(b, "prepared", 1))
                    v.wait_ge(S["params"], 16 * NPAR)
                    are, aim, ldt = sm8(0), sm8(1), sm8(2)
                    dt, lre, mag = sm8(3), sm8(4), sm8(5)
                    exp8(dt, ldt, -87.0, 88.0)
                    exp8(lre, are, -87.0, 88.0)
                    link(v.tensor_scalar(lre, lre, -1.0, None, ALU.mult))
                    link(v.tensor_tensor(sm8(6), lre, dt, ALU.mult))
                    exp8(mag, sm8(6), -87.0, 88.0)
                    gathered(upto(b, "prepared", 2))
                    th, n, mq, r, r2 = sm8(7), sm8(8), sm8(9), sm8(10), sm8(11)
                    sn, cs, sq, cq = sm8(12), sm8(13), sm8(14), sm8(15)
                    link(v.tensor_tensor(th, aim, dt, ALU.mult))
                    link(v.tensor_scalar(n, th, 2.0 / math.pi, None, ALU.mult))
                    link(v.tensor_scalar(n, n, 12582912.0, None, ALU.add))
                    link(v.tensor_scalar(n, n, 12582912.0, None, ALU.subtract))
                    link(v.scalar_tensor_tensor(r, n, -1.5703125, th, ALU.mult, ALU.add))
                    link(v.scalar_tensor_tensor(r, n, -4.8375129699707031e-4, r, ALU.mult, ALU.add))
                    link(v.scalar_tensor_tensor(r, n, -7.5497899548918e-8, r, ALU.mult, ALU.add))
                    link(v.tensor_tensor(r2, r, r, ALU.mult))
                    link(v.tensor_scalar(sn, r2, 2.7557319e-6, -1.9841270e-4, ALU.mult, ALU.add))
                    for c in (8.3333333e-3, -0.16666667):
                        link(v.tensor_tensor(sn, sn, r2, ALU.mult))
                        link(v.tensor_scalar(sn, sn, c, None, ALU.add))
                    link(v.tensor_tensor(sn, sn, r2, ALU.mult))
                    link(v.scalar_tensor_tensor(sn, sn, 1.0, r, ALU.mult, ALU.mult))
                    link(v.tensor_tensor(sn, sn, r, ALU.add))
                    link(v.tensor_scalar(cs, r2, 2.4801587e-5, -1.3888889e-3, ALU.mult, ALU.add))
                    for c in (4.1666667e-2, -0.5, 1.0):
                        link(v.tensor_tensor(cs, cs, r2, ALU.mult))
                        link(v.tensor_scalar(cs, cs, c, None, ALU.add))
                    gathered(upto(b, "prepared", 3))
                    link(v.tensor_scalar(mq, n, 0.25, None, ALU.mult))
                    link(v.tensor_scalar(mq, mq, 12582912.0, None, ALU.add))
                    link(v.tensor_scalar(mq, mq, 12582912.0, None, ALU.subtract))
                    link(v.scalar_tensor_tensor(mq, mq, -4.0, n, ALU.mult, ALU.add))
                    link(v.scalar_tensor_tensor(cq, mq, -1.0, mq, ALU.mult, ALU.min))
                    link(v.tensor_scalar(sq, cq, 2.0, None, ALU.add))
                    link(v.tensor_tensor(sq, sq, mq, ALU.mult))
                    link(v.tensor_scalar(cq, cq, 1.0, None, ALU.add))
                    cr, ci, t1, t2 = sm8(16), sm8(17), sm8(18), sm8(19)
                    link(v.tensor_tensor(t1, cq, cs, ALU.mult))
                    link(v.tensor_tensor(t2, sq, sn, ALU.mult))
                    link(v.tensor_tensor(cr, t1, t2, ALU.subtract))
                    link(v.tensor_tensor(t1, sq, cs, ALU.mult))
                    link(v.tensor_tensor(t2, cq, sn, ALU.mult))
                    link(v.tensor_tensor(ci, t1, t2, ALU.add))
                    gathered(upto(b, "prepared", 4))
                    C3 = cosT[:, :].rearrange("p (m t) -> p m t", m=8)
                    S3 = sinT[:, :].rearrange("p (m t) -> p m t", m=8)
                    T1 = wk[:, 2560:3072].rearrange("p (m t) -> p m t", m=8)
                    T2 = wk[:, 3072:3584].rearrange("p (m t) -> p m t", m=8)
                    link(v.tensor_copy(C3[:, :, 0:1], cr.unsqueeze(2)))
                    link(v.tensor_copy(S3[:, :, 0:1], ci.unsqueeze(2)))
                    n = 1
                    while n < T:
                        cb = C3[:, :, n - 1:n].broadcast_to([128, 8, n])
                        sb_ = S3[:, :, n - 1:n].broadcast_to([128, 8, n])
                        link(v.tensor_tensor(T1[:, :, 0:n], C3[:, :, 0:n], cb, ALU.mult))
                        link(v.tensor_tensor(T2[:, :, 0:n], S3[:, :, 0:n], sb_, ALU.mult))
                        link(v.tensor_tensor(C3[:, :, n:2 * n], T1[:, :, 0:n], T2[:, :, 0:n], ALU.subtract))
                        link(v.tensor_tensor(T1[:, :, 0:n], C3[:, :, 0:n], sb_, ALU.mult))
                        link(v.tensor_tensor(T2[:, :, 0:n], S3[:, :, 0:n], cb, ALU.mult))
                        link(v.tensor_tensor(S3[:, :, n:2 * n], T1[:, :, 0:n], T2[:, :, 0:n], ALU.add))
                        n *= 2
                        if n in (16, 64):
                            gathered(upto(b, "prepared", 5 + (n == 64)))
                    gathered(upto(b, "prepared", 7))
                    pp, qq, den, fre, fim = sm8(20), sm8(21), sm8(22), sm8(23), sm8(28)
                    link(v.tensor_tensor(pp, mag, cr, ALU.mult))
                    link(v.tensor_scalar(pp, pp, 1.0, None, ALU.subtract))
                    link(v.tensor_tensor(qq, mag, ci, ALU.mult))
                    link(v.tensor_tensor(t1, lre, lre, ALU.mult))
                    link(v.tensor_tensor(t2, aim, aim, ALU.mult))
                    link(v.tensor_tensor(den, t1, t2, ALU.add))
                    link(v.reciprocal(den, den))
                    link(v.tensor_tensor(t1, pp, lre, ALU.mult))
                    link(v.tensor_tensor(t2, qq, aim, ALU.mult))
                    link(v.tensor_tensor(fre, t1, t2, ALU.add))
                    link(v.tensor_tensor(fre, fre, den, ALU.mult))
                    link(v.tensor_tensor(t1, qq, lre, ALU.mult))
                    link(v.tensor_tensor(t2, pp, aim, ALU.mult))
                    link(v.tensor_tensor(fim, t1, t2, ALU.subtract))
                    link(v.tensor_tensor(fim, fim, den, ALU.mult))

                    gathered(upto(b, "prepared", 8))

                    def by8(x):
                        return x.unsqueeze(2).broadcast_to([128, 8, 16])

                    def v3(x):
                        return x.rearrange("p (m h) -> p m h", m=8)
                    br, bi = v3(wk[:, 0:128]), v3(wk[:, 128:256])
                    bbr, bbi, tb = v3(wk[:, 256:384]), v3(wk[:, 384:512]), v3(wk[:, 1920:2048])
                    link(v.tensor_tensor(bbr, br, by8(fre), ALU.mult))
                    link(v.tensor_tensor(tb, bi, by8(fim), ALU.mult))
                    link(v.tensor_tensor(bbr, bbr, tb, ALU.subtract))
                    link(v.tensor_tensor(bbi, bi, by8(fre), ALU.mult))
                    link(v.tensor_tensor(tb, br, by8(fim), ALU.mult))
                    link(v.tensor_tensor(bbi, bbi, tb, ALU.add))
                    link(v.memset(wk[:, 512:1024], 0.0))
                    for src, at in ((bbr, 512), (bbi, 768)):
                        e5 = wk[:, at:at + 256].rearrange("p (j q g h) -> p j q g h", j=2, q=4, g=2)
                        s5 = src.rearrange("p (q j) h -> p j q h", j=2)
                        for gg in range(2):
                            lo = 64 * gg
                            note(v.tensor_copy(e5[lo:lo + 64, :, :, gg, :], s5[lo:lo + 64]))
                    for at, to in ((1024, 1280), (1152, 1536)):
                        for gg, msk in ((0, EVEN), (1, ODD)):
                            c4 = wk[:, to:to + 256].rearrange("p (j g n) -> p j g n", j=2, g=2)[:, :, gg, :]
                            s4 = wk[:, at:at + 128].rearrange("p (j n) -> p j n", j=2)
                            note(v.tensor_scalar(c4, s4, col(msk), None, ALU.mult))
                    settled()
                    v.tensor_copy(m8[:, :], mag).then_inc(S["e_ready"], 1)
                    gathered(upto(b, "prepared", 9))
                    v.wait_ge(S["mod_sb"], 6)
                    v.wait_ge(S["e_ps"], 1)
                    note(v.tensor_copy(BBre[:, :], pw[:, 0:256]))
                    note(v.tensor_copy(BBim[:, :], pw[:, 256:512]))
                    note(v.tensor_copy(CCre[:, :], pw[:, 512:768]))
                    note(v.tensor_scalar(nCre[:, :], pw[:, 512:768], -1.0, None, ALU.mult))
                    note(v.tensor_scalar(nCim[:, :], pw[:, 768:1024], -1.0, None, ALU.mult))
                    note(v.tensor_copy(wsT[:, :], pw[:, 1024:1536]))
                    note(v.tensor_copy(kT[:, :], pw[:, 1536:1664]))
                    settled()
                    link(v.memset(wsT[64:128, :].rearrange("p (h t) -> p h t", h=4)[:, :, 0:64], 0.0))
                    link(v.tensor_scalar(cols[:, BGH:BGH + 2], cols[:, BGH:BGH + 2], 0.5, None, ALU.mult))
                    link(v.memset(state[:, :], 0.0))
                    link(v.memset(col(B128), 0.0))
                    link(v.tensor_scalar(col(LIMP), col(HALF), 64.0, 64.0, ALU.mult, ALU.add))
                    link(v.tensor_tensor(col(LIMP), col(LIMP), col(PCOL), ALU.subtract))
                    gained(SCALE1, hh[:, :], 1)

                def spread_c():
                    return cols[:, EVEN - 8:EVEN].unsqueeze(2).broadcast_to([128, KT, 128])

                def gained(i, gain, count):
                    v.scalar_tensor_tensor(mod(i), mod(i), 1.0, gain, ALU.add, ALU.mult).then_inc(S["gained"], 1)
                    v.wait_ge(S["gained"], count)

                def mod(i, c0=0, n=D):
                    return modb[:, i * D + c0:i * D + c0 + n]

                def normed(ss, rs, scale, shift, ready):
                    link(v.tensor_scalar(col(ss), col(ss), 1.0 / D, EPS, ALU.mult, ALU.add))
                    rsqrt(col(rs), col(ss), it[:, 2:3])
                    link(v.scalar_tensor_tensor(hh[:, :], xs[:, :], col(rs), mod(scale), ALU.mult, ALU.mult))
                    v.tensor_tensor(hh[:, :], hh[:, :], mod(shift), ALU.add).then_inc(S[ready], 1)

                def mixer():
                    if is_first(b):
                        parameters()
                    else:
                        link(v.tensor_scalar(col(B128), col(B128), 128.0, None, ALU.add))
                        link(v.tensor_scalar(col(LIMP), col(LIMP), 128.0, None, ALU.add))
                    gathered(3)
                    v.wait_ge(S["ss1"], 1)
                    normed(SS1, RS1, SCALE1, SHIFT1, "h_ready")
                    gathered(upto(b, "projected", 1))
                    v.wait_ge(S["bu_ps"], 1)
                    pq = pw[:, :].rearrange("p (q r x) -> p q r x", q=4, r=2)
                    bre, bim = pq[:, :, 0, :], pq[:, :, 1, :]

                    def q4(x):
                        return x.rearrange("p (q x) -> p q x", q=4)
                    t1, t2, t3, t4 = (wk[:, i * D:(i + 1) * D] for i in range(4))
                    cosq, sinq = q4(cosT[:, :]), q4(sinT[:, :])
                    note(v.tensor_tensor(q4(t1), bre, cosq, ALU.mult))
                    note(v.tensor_tensor(q4(t2), bim, sinq, ALU.mult))
                    note(v.tensor_tensor(q4(t3), bim, cosq, ALU.mult))
                    settled()
                    v.tensor_tensor(q4(t4), bre, sinq, ALU.mult).then_inc(S["bu_used"], 1)
                    note(v.tensor_tensor(t1, t1, t2, ALU.add))
                    v.wait_ge(S["bu_used"], 1)
                    link(v.tensor_tensor(t3, t3, t4, ALU.subtract))
                    gathered(upto(b, "projected", 2))
                    for m in range(8):
                        ms = slice(m * 128, (m + 1) * 128)
                        mg = m8[:, m:m + 1].broadcast_to([128, 128])
                        note(v.tensor_tensor_scan(t2[:, ms], mg, t1[:, ms], state[:, m:m + 1], ALU.mult, ALU.add))
                        note(v.tensor_tensor_scan(t4[:, ms], mg, t3[:, ms], state[:, 8 + m:9 + m], ALU.mult, ALU.add))
                    settled()
                    gathered(upto(b, "projected", 3))
                    note(v.tensor_tensor(t1, t2, cosT[:, :], ALU.mult))
                    note(v.tensor_tensor(t3, t4, sinT[:, :], ALU.mult))
                    settled()
                    note(v.tensor_tensor(t2, t2, sinT[:, :], ALU.mult))
                    link(v.tensor_tensor(t4, t4, cosT[:, :], ALU.mult))

                    def last(x):
                        return x.rearrange("p (m t) -> p m t", m=8)[:, :, T - 1]
                    v.tensor_tensor(state[:, 0:8], last(t1), last(t3), ALU.subtract).then_inc(S["state_re"], 1)
                    v.tensor_tensor(state[:, 8:16], last(t2), last(t4), ALU.add).then_inc(S["prods"], 1)
                    v.wait_ge(S["y_ps"], 1)
                    v.wait_ge(S["proj_sb"], 3)
                    vb, vc, sq = pr[:, 512:768], wk[:, 1024:1280], wk[:, 1280:1536]

                    def h4(x):
                        return x.rearrange("p (h d) -> p h d", h=4)

                    def bc4(x):
                        return x.unsqueeze(2).broadcast_to([128, 4, 64])
                    link(v.tensor_reduce(col(MU, 4), h4(vb), AXX, ALU.add))
                    link(v.tensor_scalar(col(MU, 4), col(MU, 4), 1.0 / 64, None, ALU.mult))
                    link(v.tensor_tensor(h4(vc), h4(vb), bc4(col(MU, 4)), ALU.subtract))
                    link(v.tensor_tensor(sq, vc, vc, ALU.mult))
                    link(v.tensor_reduce(col(V5, 4), h4(sq), AXX, ALU.add))
                    ckv = pr[:, 1280:1408]
                    link(v.tensor_tensor_reduce(out=wk[:, 1536:1664], in0=ckv, in1=ckv, scale=1.0, scalar=0.0,
                                                op0=ALU.mult, op1=ALU.add, accum_out=col(V5 + 4)))
                    note(v.tensor_scalar(col(V5, 4), col(V5, 4), 1.0 / 64, EPS, ALU.mult, ALU.add))
                    link(v.tensor_scalar(col(V5 + 4), col(V5 + 4), 1.0 / RANK, EPS, ALU.mult, ALU.add))
                    rsqrt(col(R5, 5), col(V5, 5), it[:, 3:8])
                    v.tensor_tensor(h4(vc), h4(vc), bc4(col(R5, 4)), ALU.mult).then_inc(S["vn_ready"], 1)
                    v.scalar_tensor_tensor(wk[:, 1664:1792], ckv, col(R5 + 4), kvg[:, :], ALU.mult, ALU.mult).then_inc(S["ckvn_ready"], 1)
                    gathered(upto(b, "states"))
                    v.wait_ge(S["g_ps"], 1)
                    v.tensor_tensor(mixT[:, 256:512], pj[1][:, 0:256], pr[:, 256:512], ALU.mult).then_inc(S["mix_ready"], 1)
                    y, yt = wk[:, 0:256], wk[:, 256:512]
                    for j in range(2):
                        js = slice(j * 128, (j + 1) * 128)
                        note(v.scalar_tensor_tensor(y[:, js], pr[:, js], col(DSK + j), pj[0][:, js], ALU.mult, ALU.add))
                    settled()
                    link(v.tensor_tensor(yt, y, y, ALU.mult))
                    link(v.tensor_scalar(yt, yt, GELU_A, 1.0, ALU.mult, ALU.add))
                    v.tensor_tensor(yt, yt, y, ALU.mult).then_inc(S["glu_in"], 1)
                    v.wait_ge(S["glu_th"], 1)
                    link(v.scalar_tensor_tensor(y, yt, 1.0, y, ALU.add, ALU.mult))
                    v.tensor_scalar(y, y, 0.5, None, ALU.mult).then_inc(S["yg_ready"], 1)
                    gathered(upto(b, "gated"))
                    v.wait_ge(S["z_th"], 2)
                    link(v.scalar_tensor_tensor(yt, wk[:, 512:768], 1.0, y, ALU.add, ALU.mult))
                    v.tensor_scalar(mixT[:, 0:256], yt, 0.5, None, ALU.mult).then_inc(S["mix_ready"], 1)
                    if is_first(b):
                        v.wait_ge(S["proj_ps"], 4)
                        v.tensor_copy(hT[:, :].rearrange("p (k m) -> p k m", k=KT), spread_c()).then_inc(S["crep_ready"], 1)
                    v.wait_ge(S["ckv_cached"], 2)
                    sc, am, nd, D_ = wk[:, 0:512], wk[:, 1024:1536], wk[:, 1536:2048], wk[:, 512:1024]
                    note(v.tensor_scalar(col(WSC, 4), pr[:, 1792:1796], 1.0 / 16, None, ALU.mult))
                    note(v.tensor_scalar(am, nd0[:, :], col(LIMP), NEG, ALU.is_ge, ALU.mult))
                    note(v.tensor_scalar(nd, nd0[:, :], col(B128), None, ALU.subtract))
                    settled()
                    link(v.scalar_tensor_tensor(nd, nd, -1.0, nd, ALU.mult, ALU.min))
                    v.wait_ge(S["relu_sb"], 1)
                    link(v.tensor_scalar(sc, wk[:, 2048:2560], col(WSC), None, ALU.mult))
                    for h in range(1, IH):
                        v.wait_ge(S["relu_sb"], h + 1)
                        link(v.scalar_tensor_tensor(sc, wk[:, 2048 + h * 512:2560 + h * 512], col(WSC + h), sc, ALU.mult, ALU.add))
                    v.tensor_tensor(sc, sc, am, ALU.add).then_inc(S["scored"], 1)
                    v.wait_ge(S["scored"], 1)
                    link(v.tensor_tensor(nd, am, nd, ALU.add))
                    gathered(upto(b, "gated") + 1)
                    for r in range(TOPK // 8):
                        link(v.max(val[:, 0:8], sc))
                        link(v.match_replace(sc, val[:, 0:8], sc, GONE))
                        gathered(upto(b, "picked", r))
                    link(v.tensor_scalar(D_, sc, -2e38, NEG, ALU.is_gt, ALU.mult))
                    link(v.tensor_tensor(D_, D_, nd, ALU.add))
                    if is_first(b):
                        v.wait_ge(S["mod_sb"], 10)
                        v.wait_ge(S["gain2_in"], 16)
                        gained(SCALE2, wk[:, 3 * D:4 * D], 2)

                    def scale_p(h):
                        v.wait_ge(S["exp_done"], h + 1)
                        link(v.reciprocal(col(RD + h), col(DEN + h)))
                        P = wk[:, 3072 + (h % 2) * 512:3584 + (h % 2) * 512]
                        v.tensor_scalar(P, P, col(RD + h), None, ALU.mult).then_inc(S["p_ready"], 1)
                    for h in range(AH):
                        v.wait_ge(S["lg_ps"], h + 1)
                        if h >= 2:
                            v.wait_ge(S["exp_done"], h - 1)
                        L = wk[:, 2048 + (h % 2) * 512:2560 + (h % 2) * 512]
                        v.scalar_tensor_tensor(L, D_, 2.0 ** (-8.0 * (h + 1) / AH), pw[:, (h % 2) * 512:(h % 2 + 1) * 512],
                                               ALU.mult, ALU.add).then_inc(S["lg_used"], 1)
                        v.wait_ge(S["lg_used"], h + 1)
                        v.tensor_reduce(col(NM + h), L, AXX, ALU.max, negate=True).then_inc(S["nmax"], 1)
                        if h >= 1:
                            scale_p(h - 1)
                        gathered(upto(b, "heads", h))
                    scale_p(AH - 1)
                    gathered(upto(b, "values"))
                    for n in range(2):
                        v.wait_ge(S["out_ps"], n + 1)
                        ns = slice(n * 512, (n + 1) * 512)
                        link(v.tensor_tensor(wk[:, ns], pj[n][:, :], mod(GATE1, n * 512, 512), ALU.mult))
                        v.tensor_tensor(xs[:, ns], xs[:, ns], wk[:, ns], ALU.add).then_inc(S["x1_ready"], 1)
                    v.wait_ge(S["x1_ready"], 2)
                    gathered(upto(b, "x1"))
                    v.wait_ge(S["ss2"], 1)
                    normed(SS2, RS2, SCALE2, SHIFT2, "h2_ready")
                    gathered(upto(b, "queries", 1) + 1)
                    v.wait_ge(S["s_ps"], 1)
                    s16 = pw[:, :].rearrange("p (f n) -> p f n", f=16)
                    r16 = wk[:, 2048:4096].rearrange("p (f n) -> p f n", f=16)
                    v16 = val[:, :].rearrange("p (f k) -> p f k", f=16)
                    i16 = vix[:, :].rearrange("p (f k) -> p f k", f=16)
                    for f in range(16):
                        note(v.max(v16[:, f, 0:8], s16[:, f, :]))
                    settled()
                    for f in range(16):
                        note(v.max_index(i16[:, f, 0:8], v16[:, f, 0:8], s16[:, f, :]))
                        note(v.match_replace(r16[:, f, :], v16[:, f, 0:8], s16[:, f, :], GONE))
                        if f % 8 == 7:
                            gathered(upto(b, "routing", f // 8))
                    settled()
                    for f in range(16):
                        note(v.max(v16[:, f, 8:16], r16[:, f, :]))
                    settled()
                    for f in range(16):
                        note(v.max_index(i16[:, f, 8:16], v16[:, f, 8:16], r16[:, f, :]))
                    settled()
                    gathered(upto(b, "routing", 2))
                    cand = wk[:, 0:2048].rearrange("p (h a b) -> p h a b", h=8, a=16)
                    va = val[:, 0:128].unsqueeze(2).broadcast_to([128, 128, 16]).rearrange("p (h a) b -> p h a b", h=8)
                    vb2 = val[:, 128:256].rearrange("p (h b) -> p h b", h=8).unsqueeze(2).broadcast_to([128, 8, 16, 16])
                    for h in range(PH):
                        note(v.tensor_tensor(cand[:, h], va[:, h], vb2[:, h], ALU.add))
                    settled()
                    c8 = wk[:, 0:2048].rearrange("p (h c) -> p h c", h=8)
                    d8 = wk[:, 2048:4096].rearrange("p (h c) -> p h c", h=8)
                    cv8 = cv[:, :].rearrange("p (h k) -> p h k", h=8)
                    cp8 = cpos[:, :].rearrange("p (h k) -> p h k", h=8)
                    for h in range(PH):
                        note(v.max(cv8[:, h, 0:8], c8[:, h, :]))
                    settled()
                    for h in range(PH):
                        note(v.max_index(cp8[:, h, 0:8], cv8[:, h, 0:8], c8[:, h, :]))
                        note(v.match_replace(d8[:, h, :], cv8[:, h, 0:8], c8[:, h, :], GONE))
                    settled()
                    gathered(upto(b, "routing", 3))
                    for h in range(PH):
                        note(v.max(cv8[:, h, 8:16], d8[:, h, :]))
                    settled()
                    for h in range(PH):
                        note(v.max_index(cp8[:, h, 8:16], cv8[:, h, 8:16], d8[:, h, :]))
                    settled()
                    gathered(upto(b, "routing", 4))
                    gw8 = gate_w[:, :].rearrange("p (h k) -> p h k", h=8)
                    v.tensor_tensor(gw8, cv8, cv8[:, :, 0:1].broadcast_to([128, 8, 16]), ALU.subtract).then_inc(S["top_ready"], 1)
                    pa, pb = hT[:, 768:896].bitcast(I32), hT[:, 896:1024].bitcast(I32)
                    af, bf, ixf = hT[:, 0:128], hT[:, 128:256], hT[:, 256:512]
                    e1, e2 = hT[:, 512:640], hT[:, 640:768]
                    cpi = cpos[:, :].bitcast(I32)
                    note(v.tensor_scalar(pa, cpi, 4, None, ALU.logical_shift_right))
                    note(v.tensor_scalar(pb, cpi, 15, None, ALU.bitwise_and))
                    note(v.tensor_copy(ixf, vix[:, :]))
                    settled()
                    note(v.tensor_copy(af, pa))
                    note(v.tensor_copy(bf, pb))
                    settled()
                    eq = wk[:, 0:2048].rearrange("p (e a) -> p e a", e=128)
                    eq4 = wk[:, 0:2048].rearrange("p (h j a) -> p h j a", h=8, j=16)
                    for src, half, dst in ((af, 0, e1), (bf, 1, e2)):
                        link(v.tensor_tensor(eq, src.unsqueeze(2).broadcast_to([128, 128, 16]),
                                             iota16[:, :].unsqueeze(1).broadcast_to([128, 128, 16]), ALU.is_equal))
                        keys = ixf[:, half * 128:(half + 1) * 128].rearrange("p (h a) -> p h a", h=8)
                        link(v.tensor_tensor(eq4, eq4, keys.unsqueeze(2).broadcast_to([128, 8, 16, 16]), ALU.mult))
                        link(v.tensor_reduce(dst, eq, AXX, ALU.add))
                        gathered(upto(b, "routing", 5))
                    link(v.tensor_scalar(e1, e1, float(NKEY), float(l * NEXP), ALU.mult, ALU.add))
                    link(v.tensor_tensor(e1, e1, e2, ALU.add))
                    link(v.tensor_copy(idx_w[:, :], e1))
                    v.wait_ge(S["gexp"], 1)
                    link(v.tensor_reduce(cols[:, V5:V5 + 8], gw8, AXX, ALU.add))
                    link(v.reciprocal(cols[:, V5:V5 + 8], cols[:, V5:V5 + 8]))
                    link(v.tensor_scalar(cols[:, V5:V5 + 8], cols[:, V5:V5 + 8], 0.5, None, ALU.mult))
                    v.tensor_tensor(gw8, gw8, cols[:, V5:V5 + 8].unsqueeze(2).broadcast_to([128, 8, 16]), ALU.mult).then_inc(S["routed"], 1)
                    v.wait_ge(S["routed"], 1)

                if mixers:
                    mixer()
                gathered(NBAT + 1)
                if g is not None:
                    v.wait_ge(S["mixed"], HK)
                    v.wait_ge(S["x1_loaded"], 16)
                    link(v.tensor_tensor(wk[:, 0:D], py[:, :], g2g[:, :], ALU.mult))
                    if g[0] < DEPTH - 1:
                        v.tensor_tensor(wk[:, D:2 * D], wk[:, 0:D], wk[:, 3 * D:4 * D], ALU.add).then_inc(S["xn_ready"], 1)
                    else:
                        link(v.tensor_tensor(wk[:, D:2 * D], wk[:, 0:D], wk[:, 3 * D:4 * D], ALU.add))
                        xn = wk[:, D:2 * D]
                        link(v.tensor_tensor_reduce(out=wk[:, 0:D], in0=xn, in1=xn, scale=1.0, scalar=0.0,
                                                    op0=ALU.mult, op1=ALU.add, accum_out=col(SS1)))
                        link(v.tensor_scalar(col(SS1), col(SS1), 1.0 / D, EPS, ALU.mult, ALU.add))
                        rsqrt(col(RS1), col(SS1), it[:, 2:3])
                        v.wait_ge(S["gain_in"], 16)
                        v.scalar_tensor_tensor(wk[:, D:2 * D], xn, col(RS1), wk[:, 2 * D:3 * D], ALU.mult,
                                               ALU.mult).then_inc(S["xn_ready"], 1)
                if mixers:
                    note(v.tensor_copy(h2g[:, :], hh[:, :]))
                    note(v.tensor_copy(g2g[:, :], mod(GATE2)))
                    note(v.tensor_copy(gate_g[:, :], gate_w[:, :]))
                    note(v.tensor_copy(idx_g[:, :], idx_w[:, :]))
                meet(v, "dve")
            legs(v, leg)

        @block.sync
        def _(sp):
            sp.wait_ge(consts, 16)

            def bcast(row, n=128):
                return row.partition_broadcast(n)

            def leg(l, b, mixers, g, before):
                wn = [0 if is_first(b) else 2]
                users = [("proj_ps", i + 1) for i in range(4)]
                if is_first(b):
                    users = ([("mod_ps", i + 1) for i in range(MOD_EARLY)] + users
                             + [("mod_ps", i + 1) for i in range(MOD_EARLY, 12)])
                users += [("out_ps", 1), ("out_ps", 2), ("pq_ps", 1), ("pq_ps", 2)]

                def weights(src, c0, width):
                    n = wn[0]
                    wn[0] += 1
                    if n >= 2:
                        sem, count = users[n - 2]
                        sp.wait_ge(S[sem], count)
                    sp.dma_start(wring[n % 2][:, 0:KT * width].rearrange("p (k c) -> p k c", k=KT),
                                 src.rearrange("(k p) c -> p k c", p=128)[:, :, c0:c0 + width]).then_inc(S[f"w_l{n % 2}"], 16)

                if mixers:
                    if is_first(b):
                        sp.dma_start(sm[:, 312:320], A["c"].rearrange("o (k p) -> p (o k)", p=128),
                                     allow_slow_non_contiguous=True).then_inc(S["c_loaded"], 16)
                        sp.dma_start(modb[0:1, :], A["b_mod"][l].rearrange("(o n) -> o n", o=1)).then_inc(S["b_loaded"], 16)
                    src = A["x"].rearrange("o s d -> (o s) d") if l == 0 else x_mid
                    sp.dma_start(xs[:, :], src[bass.ds(b * T, T), :]).then_inc(S["x_in"], 16)
                    if is_first(b):
                        for n in range(MOD_EARLY):
                            weights(A["w_mod"][l], n * 512, 512)
                    for c0, width in GROUPS if is_first(b) else GROUPS[2:]:
                        weights(A["w_in"][l], c0, width)
                    if is_first(b):
                        for n in range(MOD_EARLY, 12):
                            weights(A["w_mod"][l], n * 512, 512)
                        sp.wait_ge(S["scored"], 1)
                        sp.dma_start(wk[:, 3 * D:4 * D], bcast(A["norm2_g"][l])).then_inc(S["gain2_in"], 16)
                    for name in ("w_out", "peer_w_q"):
                        for n in range(2):
                            weights(A[name][l], n * 512, 512)
                    sp.wait_ge(S["x1_ready"], 2)
                    sp.dma_start(x_mix[bass.ds(b * T, T), :], xs[:, :]).then_inc(S["x1_saved"], 16)
                    for c0, width in GROUPS[:2]:
                        weights(A["w_in"][l], c0, width)
                if g is not None:
                    gl, gb = g
                    if mixers:
                        sp.wait_ge(S["routed"], 1)
                    sp.dma_start(wk[:, 3 * D:4 * D], x_mix[bass.ds(gb * T, T), :]).then_inc(S["x1_loaded"], 16)
                    if gl == DEPTH - 1:
                        sp.dma_start(wk[:, 2 * D:3 * D], bcast(A["final_g"])).then_inc(S["gain_in"], 16)
                    sp.wait_ge(S["xn_ready"], 1)
                    dst = (out.rearrange("o s d -> (o s) d") if gl == DEPTH - 1 else x_mid)[bass.ds(gb * T, T), :]
                    sp.dma_start(dst, wk[:, D:2 * D]).then_inc(S["x_stored"], 16)
                    sp.wait_ge(S["x_stored"], 16)
                if mixers:
                    sp.wait_ge(S["x1_saved"], 16)
                    for i in range(2):
                        sp.wait_ge(S[f"w_l{i}"], 16 * ((wn[0] - (0 if is_first(b) else 2)) // 2))
                sp.wait_ge(arrive, 4)
                sp.sem_inc(arrive, -4)
                sp.sem_clear(range(nums[0], nums[-1] + 1))
                for s in go.values():
                    sp.sem_inc(s, 1)
            legs(sp, leg)


_INS = ["x", "c", "norm1_g", "norm2_g", "w_mod", "b_mod", "w_in", "ssm_a_re_log", "ssm_a_im", "ssm_b_re",
        "ssm_b_im", "ssm_c_re", "ssm_c_im", "ssm_d", "ssm_log_dt", "ssm_w_glu", "ssm_b_glu", "gmlp_w_sp",
        "gmlp_b_sp", "kv_norm_g", "w_uk", "w_uv", "w_out", "peer_w_q", "peer_k1", "peer_k2", "peer_u",
        "peer_v", "final_g"]


def kernel(**inputs):
    import numpy as np
    import concourse.bacc as bacc
    from concourse.bass_utils import run_bass_kernel_spmd

    nc = bacc.Bacc("TRN2", target_bir_lowering=False, num_devices=1)
    arrays, A = {}, {}
    for name in _INS:
        a = np.ascontiguousarray(inputs[name])
        arrays[f"in_{name}"] = a
        A[name] = nc.dram_tensor(f"in_{name}", a.shape, mybir.dt.from_np(a.dtype), kind="ExternalInput").ap()
    out = nc.dram_tensor("out", (1, SEQ, D), F32, kind="ExternalOutput").ap()
    build(nc, A, out)
    r = run_bass_kernel_spmd(nc, [arrays], core_ids=[0])
    return r.results[0]["out"]
```
